# Optimizing a Trainium2 kernel written in Bass

```python
import math
import jax, jax.numpy as jnp
from jax import lax
import numpy as np

D_MODEL = 2048
BATCH = 1
SEQ = 512
DEPTH = 1

P_DIM = 256
CONV_CH = 1024
CONV_WIDTH = 31
ATTN_HEADS = 8
ATTN_HEAD_DIM = 64
ATTN_V_DIM = 2 * ATTN_HEAD_DIM
Q_BLOCK = 128
N_BRANCHES = 2
PEER_HEADS = 8
PEER_N_KEYS = 128
PEER_N_EXPERTS = PEER_N_KEYS * PEER_N_KEYS
PEER_KEY_DIM = 256
PEER_HALF = PEER_KEY_DIM // 2
PEER_TOPK = 16
TOKEN_BLOCK = 128
LN_EPS = 1e-5
ALPHA = (2.0 * DEPTH) ** 0.25
BETA = (8.0 * DEPTH) ** -0.25

COL_CONV = 2 * CONV_CH
COL_Q = ATTN_HEADS * 2 * ATTN_HEAD_DIM
COL_K = ATTN_HEADS * 2 * ATTN_HEAD_DIM
COL_V = ATTN_HEADS * ATTN_V_DIM
COL_GATE = N_BRANCHES * D_MODEL
IN_COLS = COL_CONV + COL_Q + COL_K + COL_V + COL_GATE
SPLITS = (COL_CONV, COL_CONV + COL_Q, COL_CONV + COL_Q + COL_K, COL_CONV + COL_Q + COL_K + COL_V)

kernel_name = "hybrid_conv_diffattn_peer_deepnorm"

def lambda_init(layer_idx):
    return 0.8 - 0.6 * math.exp(-0.3 * layer_idx)

def layer_norm(x, g, b):
    xf = x.astype(jnp.float32)
    mu = jnp.mean(xf, axis=-1, keepdims=True)
    var = jnp.mean(jnp.square(xf - mu), axis=-1, keepdims=True)
    return ((xf - mu) * lax.rsqrt(var + LN_EPS)).astype(x.dtype) * g + b

def rms_norm(x, g):
    xf = x.astype(jnp.float32)
    ms = jnp.mean(jnp.square(xf), axis=-1, keepdims=True)
    return (xf * lax.rsqrt(ms + LN_EPS)).astype(x.dtype) * g

def alibi_slopes():
    return jnp.asarray(2.0 ** (-8.0 * np.arange(1, ATTN_HEADS + 1) / ATTN_HEADS), dtype=jnp.float32)

def conformer_conv(a, dw_w, dw_b, ln_g, ln_b, w_pw):
    h = a[..., :CONV_CH] * jax.nn.sigmoid(a[..., CONV_CH:])
    h = lax.conv_general_dilated(
        h, dw_w.astype(h.dtype), window_strides=(1,), padding=[(CONV_WIDTH - 1, 0)],
        dimension_numbers=('NWC', 'WIO', 'NWC'), feature_group_count=CONV_CH) + dw_b
    h = layer_norm(h, ln_g, ln_b)
    h = jax.nn.silu(h)
    return h @ w_pw

def diff_attention(q, k, v, lam, lam_init, subln_g, w_o, slopes):
    B, S, _ = q.shape
    nb = S // Q_BLOCK
    scale = ATTN_HEAD_DIM ** -0.5
    qb = q.reshape(B, nb, Q_BLOCK, ATTN_HEADS, 2, ATTN_HEAD_DIM).transpose(1, 0, 3, 4, 2, 5)
    kh = k.reshape(B, S, ATTN_HEADS, 2, ATTN_HEAD_DIM).transpose(0, 2, 3, 1, 4)
    vh = v.reshape(B, S, ATTN_HEADS, ATTN_V_DIM).transpose(0, 2, 1, 3)
    kpos = jnp.arange(S)

    def block(args):
        qblk, bi = args
        s = jnp.einsum('bhmqd,bhmkd->bhmqk', qblk, kh).astype(jnp.float32) * scale
        qpos = bi * Q_BLOCK + jnp.arange(Q_BLOCK)
        dist = qpos[:, None] - kpos[None, :]
        bias = -slopes[:, None, None] * dist.astype(jnp.float32)[None]
        s = jnp.where((dist >= 0)[None, None, None], s + bias[None, :, None], -jnp.inf)
        pr = jax.nn.softmax(s, axis=-1)
        a = pr[:, :, 0] - lam * pr[:, :, 1]
        return jnp.einsum('bhqk,bhkv->bhqv', a.astype(vh.dtype), vh)

    o = lax.map(block, (qb, jnp.arange(nb)))
    o = o.transpose(1, 0, 3, 2, 4).reshape(B, S, ATTN_HEADS, ATTN_V_DIM)
    o = rms_norm(o, subln_g) * (1.0 - lam_init)
    return o.reshape(B, S, ATTN_HEADS * ATTN_V_DIM) @ w_o

def peer(x, w_q, sub_keys, u_tab, v_tab):
    B, S, D = x.shape
    xt = x.reshape((B * S) // TOKEN_BLOCK, TOKEN_BLOCK, D)

    def block(xb):
        q = (xb @ w_q).reshape(TOKEN_BLOCK, PEER_HEADS, 2, PEER_HALF)
        s = jnp.einsum('thcd,hcnd->thcn', q, sub_keys).astype(jnp.float32)
        vals, idx = lax.top_k(s, PEER_TOPK)
        cand = vals[:, :, 0, :, None] + vals[:, :, 1, None, :]
        cand_ids = idx[:, :, 0, :, None] * PEER_N_KEYS + idx[:, :, 1, None, :]
        best, pos = lax.top_k(cand.reshape(TOKEN_BLOCK, PEER_HEADS, PEER_TOPK * PEER_TOPK), PEER_TOPK)
        ids = jnp.take_along_axis(cand_ids.reshape(TOKEN_BLOCK, PEER_HEADS, PEER_TOPK * PEER_TOPK), pos, axis=-1)
        g = jax.nn.softmax(best, axis=-1)
        u = u_tab[ids]
        v = v_tab[ids]
        h = jax.nn.gelu(jnp.einsum('td,thkd->thk', xb, u))
        w = (g * h.astype(jnp.float32)).astype(xb.dtype)
        return jnp.einsum('thk,thkd->td', w, v)

    return lax.map(block, xt).reshape(B, S, D)

def setup_inputs(seed: int = 0) -> dict:
    key = jax.random.key(seed)
    ks = jax.random.split(key, 32)
    f32 = jnp.float32
    L, D = DEPTH, D_MODEL

    def nrm(k, shape, scale):
        return jax.random.normal(k, shape, f32) * scale

    w_in = jnp.concatenate([
        nrm(ks[2], (L, D, COL_CONV), D ** -0.5),
        nrm(ks[3], (L, D, COL_Q + COL_K), D ** -0.5),
        nrm(ks[4], (L, D, COL_V), BETA * D ** -0.5),
        nrm(ks[5], (L, D, COL_GATE), D ** -0.5),
    ], axis=-1)
    return {
        "x": nrm(ks[0], (BATCH, SEQ, D), 1.0),
        "p": nrm(ks[1], (DEPTH, BATCH, SEQ, P_DIM), 1.0),
        "w_in": w_in,
        "b_gate": nrm(ks[6], (L, COL_GATE), 0.02),
        "conv_dw_w": nrm(ks[7], (L, CONV_WIDTH, 1, CONV_CH), CONV_WIDTH ** -0.5),
        "conv_dw_b": nrm(ks[8], (L, CONV_CH), 0.02),
        "conv_ln_g": 1.0 + nrm(ks[9], (L, CONV_CH), 0.02),
        "conv_ln_b": nrm(ks[10], (L, CONV_CH), 0.02),
        "conv_w_out": nrm(ks[11], (L, CONV_CH, D), BETA * CONV_CH ** -0.5),
        "attn_lambda_q1": nrm(ks[12], (L, ATTN_HEAD_DIM), 0.1),
        "attn_lambda_k1": nrm(ks[13], (L, ATTN_HEAD_DIM), 0.1),
        "attn_lambda_q2": nrm(ks[14], (L, ATTN_HEAD_DIM), 0.1),
        "attn_lambda_k2": nrm(ks[15], (L, ATTN_HEAD_DIM), 0.1),
        "attn_subln_g": 1.0 + nrm(ks[16], (L, ATTN_V_DIM), 0.02),
        "attn_w_o": nrm(ks[17], (L, COL_V, D), BETA * COL_V ** -0.5),
        "w_out": nrm(ks[18], (L, D, D), BETA * D ** -0.5),
        "ln1_g": 1.0 + nrm(ks[19], (L, D), 0.02),
        "ln1_b": nrm(ks[20], (L, D), 0.02),
        "peer_w_q": nrm(ks[21], (L, D, PEER_HEADS * PEER_KEY_DIM), D ** -0.5),
        "peer_sub_keys": nrm(ks[22], (L, PEER_HEADS, 2, PEER_N_KEYS, PEER_HALF), PEER_HALF ** -0.5),
        "peer_u": nrm(ks[23], (L, PEER_N_EXPERTS, D), D ** -0.5),
        "peer_v": nrm(ks[24], (L, PEER_N_EXPERTS, D), BETA),
        "ln2_g": 1.0 + nrm(ks[25], (L, D), 0.02),
        "ln2_b": nrm(ks[26], (L, D), 0.02),
        "ple_w_proj": nrm(ks[27], (L, P_DIM, D), BETA * P_DIM ** -0.5),
        "ple_w_gate": nrm(ks[28], (L, D, D), D ** -0.5),
        "ple_b_gate": nrm(ks[29], (L, D), 0.02),
    }

def reference(x, p, w_in, b_gate, conv_dw_w, conv_dw_b, conv_ln_g, conv_ln_b, conv_w_out,
              attn_lambda_q1, attn_lambda_k1, attn_lambda_q2, attn_lambda_k2, attn_subln_g, attn_w_o,
              w_out, ln1_g, ln1_b, peer_w_q, peer_sub_keys, peer_u, peer_v, ln2_g, ln2_b,
              ple_w_proj, ple_w_gate, ple_b_gate):
    B, S, D = x.shape
    slopes = alibi_slopes()
    for i in range(DEPTH):
        lam_init = lambda_init(i)
        proj = x @ w_in[i]
        a_conv, q, k, v, g_logits = jnp.split(proj, SPLITS, axis=-1)
        y_conv = conformer_conv(a_conv, conv_dw_w[i], conv_dw_b[i], conv_ln_g[i], conv_ln_b[i], conv_w_out[i])
        lam = (jnp.exp(jnp.sum(attn_lambda_q1[i] * attn_lambda_k1[i]).astype(jnp.float32))
               - jnp.exp(jnp.sum(attn_lambda_q2[i] * attn_lambda_k2[i]).astype(jnp.float32)) + lam_init)
        y_attn = diff_attention(q, k, v, lam, lam_init, attn_subln_g[i], attn_w_o[i], slopes)
        gates = jax.nn.sigmoid(g_logits + b_gate[i]).reshape(B, S, N_BRANCHES, D)
        mixed = gates[:, :, 0] * y_conv + gates[:, :, 1] * y_attn
        x = layer_norm(ALPHA * x + mixed @ w_out[i], ln1_g[i], ln1_b[i])
        x = layer_norm(ALPHA * x + peer(x, peer_w_q[i], peer_sub_keys[i], peer_u[i], peer_v[i]), ln2_g[i], ln2_b[i])
        e = p[i] @ ple_w_proj[i]
        x = x + jax.nn.sigmoid(x @ ple_w_gate[i] + ple_b_gate[i]) * e
    return x


_drawn_inputs = setup_inputs


def setup_inputs(seed=0):
    import zlib

    import numpy as np

    out = dict(_drawn_inputs(seed))
    spreads = {}
    factors = {'b_gate': 5.839,
     'conv_dw_b': 3.31,
     'conv_ln_g': 4.55,
     'conv_ln_b': 5.011,
     'attn_lambda_q2': 6.65,
     'attn_subln_g': 3.994,
     'ln2_g': 2.843,
     'ln2_b': 3.023,
     'ple_b_gate': 8.0}
    for name, (base, spread) in spreads.items():
        noise = np.random.default_rng([zlib.crc32(name.encode()), seed]).standard_normal(out[name].shape)
        drawn = base * np.exp(spread * noise) if base else spread * noise
        out[name] = __import__('jax').numpy.asarray(drawn.astype(out[name].dtype))
    for name, factor in factors.items():
        out[name] = (out[name] * factor).astype(out[name].dtype)
    return out
```

```python
from contextlib import ExitStack

import concourse.bass as bass
from concourse import mybir

P = 128
F32 = mybir.dt.float32
F32R = mybir.dt.float32r
U32 = mybir.dt.uint32
ALU = mybir.AluOpType
ACT = mybir.ActivationFunctionType
AX = mybir.AxisListType

D = 2048
T = 512
TT = T // P
KD = D // P
CH = 1024
NH = 8
W = 31
NK = 128
TOPK = 16
PH = 8
ALPHA = 2.0 ** 0.25
LAM0 = 0.2
EPS = 1e-5

U1 = 8 * NH
U1T = 8
U2 = KD
U3 = KD
U4 = 2 * PH
U5 = 128
U6 = 128
U7 = 2
U8 = KD
B1 = 0
B1T = B1 + 2 * U1
B2 = B1T + 2 * U1T
B3 = B2 + 2 * U2
B4 = B3 + 2 * U3
B5 = B4 + 2 * U4
B6 = B5 + 2 * U5
B7 = B6 + 2 * U6
B8 = B7 + 2 * U7
NB = B8 + 2 * U8
NU = NB // 2
AHEAD = 4
FIRST_GATE_TAIL = 3 * NH
ROUTE0 = 5

C_BIAS, C_LNG, C_LNB, C_SLOPE, NCPAR = W, W + 1, W + 2, W + 3, W + 5
V_LN1G, V_LN1B, V_LN2G, V_LN2B, V_PLEB, V_BG, V_SUB = 0, 16, 32, 48, 64, 80, 112
NPV = 113


def build(nc, ws, xT, pT, cpar, pvec, lamT, keysT, out):
    out2 = out.rearrange("b t d -> (b t) d")
    gate_sp = nc.dram_tensor("gate_spill", (2 * KD, P, T), F32).ap()
    x1_sp = nc.dram_tensor("x1_spill", (P, KD, T), F32).ap()
    gelu_sp = nc.dram_tensor("gelu_spill", (NK, P, T), F32).ap()
    route_sp = nc.dram_tensor("route_spill", (TT, P, NK * P), F32).ap()

    with ExitStack() as ctx:
        def sem(name):
            return ctx.enter_context(nc.semaphore(name))

        KB = 1024
        base = 16512
        size = 212832 - 64
        ctx.enter_context(nc.sbuf_tensor("arena", [P, size // 4], F32))

        def at(name, offset, shape, dt=F32):
            n = 4
            for s in shape[1:]:
                n *= s
            assert offset + n <= size, (name, offset + n, size)
            return nc.alloc_sbuf_tensor_at(name, shape, dt, offset=base + offset)

        o_raw, o_whi, o_wlo, o_ahi, o_alo, o_r, o_s, o_c = [
            k * KB for k in (0, 16, 32, 48, 80, 112, 144, 176)]
        raw = at("raw", o_raw, [P, 2, 2, 1024])
        whi = at("whi", o_whi, [P, 4, 1024], F32R)
        wlo = at("wlo", o_wlo, [P, 4, 1024], F32R)
        ahi = at("ahi", o_ahi, [P, KD, T], F32R)
        alo = at("alo", o_alo, [P, KD, T], F32R)
        xin = at("xin", o_r, [P, KD, T])
        oThi = at("oThi", o_r, [P, NH, T], F32R)
        oTlo = at("oTlo", o_r + 16 * KB, [P, NH, T], F32R)
        res = at("res", o_r, [P, KD, T])
        gst = at("gst", o_r, [P, NK * P])
        swhi = at("swhi", o_s, [P, NH, T], F32R)
        conv = at("conv", o_s + 16 * KB, [P, NH, T])
        swlo = at("swlo", o_s + 16 * KB, [P, NH, T], F32R)
        xwhi = [at("xwhi0", o_s, [P, 8, T], F32R), ahi]
        xwlo = [at("xwlo0", o_s + 16 * KB, [P, 8, T], F32R), alo]
        eT = at("eT", o_s, [P, KD, T])

        c = [o_c]

        def small(name, shape, dt=F32):
            n = 4
            for s in shape[1:]:
                n *= s
            t = at(name, c[0], shape, dt)
            c[0] += (n + 31) // 32 * 32
            return t

        ident = small("ident", [P, P])
        ones = small("ones", [P, P])
        iota = small("iota", [P, NK])
        par = small("par", [P, NH, NCPAR])
        pv = small("pv", [P, NPV])
        lamv = small("lamv", [64, 4])
        lamp = small("lamp", [64, 2])
        lame = small("lame", [P, 2])
        nlam = small("nlam", [P, 1])
        sub8 = small("sub8", [P, 1])
        eps = small("eps", [P, 1])
        o_phase = c[0]

        glu = small("glu", [P, W - 1 + T])
        sg = small("sg", [P, T])
        sc = small("sc", [P, 2, T])
        aN = small("aN", [P, T])
        cur = small("cur", [P, NCPAR])
        nmx = small("nmx", [P, 2])
        sums = small("sums", [P, 2])
        rcp = small("rcp", [P, 2])
        rl = small("rl", [P, 1])
        ssq = small("ssq", [P, TT])
        rms = small("rms", [P, TT])
        rrms = small("rrms", [P, TT])
        assert c[0] <= o_phase + 12 * KB
        acc = sc[:, 0]
        o_after_ln = o_phase + 12 * KB
        c[0] = o_after_ln
        gout = small("gout", [P, 2, T])
        on = small("on", [P, T])
        oTf = small("oTf", [P, T])
        junk = small("junk", [P, P])
        c[0] = o_s
        qT = small("qT", [P, T])
        kT = small("kT", [P, T])
        vT = small("vT", [P, T])
        vn = small("vn", [P, TT, P])
        nd = small("nd", [P, T])
        aT = small("aT", [P, 2, T])
        assert c[0] <= o_s + 16 * KB

        c[0] = o_phase
        sq = small("sq", [P, 2, T])
        std = small("std", [P, T])
        rstd = small("rstd", [P, T])
        nrm = small("nrm", [P, 2, T])
        assert c[0] <= o_after_ln
        c[0] = o_after_ln
        gl = small("gl", [P, 2, 2, T])
        mt = small("mt", [P, T])
        xr = small("xr", [P, 2, T])
        assert c[0] <= size
        keys = at("keys", o_after_ln, [P, 2 * PH, NK])
        c[0] = o_phase
        s4 = small("s4", [P, TT, NK])
        s4b = small("s4b", [P, TT, NK])
        cand = small("cand", [P, TT, TOPK * TOPK])
        assert c[0] <= o_after_ln
        c[0] = o_after_ln + 8 * KB
        qs = small("qs", [P, 2, T])
        assert c[0] <= size
        c[0] = o_s
        top = small("top", [P, 2, TT, TOPK])
        topi = small("topi", [P, 2, TT, TOPK], U32)
        best = small("best", [P, TT, PH, TOPK])
        bpos = small("bpos", [P, TT, PH, TOPK], U32)
        k1f = small("k1f", [P, TT, PH, TOPK])
        k2f = small("k2f", [P, TT, PH, TOPK])
        cand2 = small("cand2", [P, TT, TOPK * TOPK])
        bnow = small("bnow", [P, TT, TOPK])
        pnow = small("pnow", [P, TT, TOPK], U32)
        pab = small("pab", [P, 2, TT, TOPK], U32)
        pabf = small("pabf", [P, 2, TT, TOPK])
        know = small("know", [P, 2, TT, TOPK])
        hot = small("hot", [P, TT, TOPK, TOPK])
        pick = small("pick", [P, TT, TOPK])
        i1n = small("i1n", [P, TT, PH, TOPK])
        i2n = small("i2n", [P, TT, PH, TOPK])
        gn = small("gn", [P, TT, PH, TOPK])
        gsum = small("gsum", [P, TT * PH])
        grcp = small("grcp", [P, TT * PH])
        assert c[0] <= o_c
        c[0] = o_phase
        i1T = small("i1T", [P, T])
        i2T = small("i2T", [P, T])
        ghi = small("ghi", [P, T], F32R)
        glo = small("glo", [P, T], F32R)
        hot1 = small("hot1", [P, 2, 4, P], F32R)
        hot2h = small("hot2h", [P, 2, 4, P], F32R)
        hot2l = small("hot2l", [P, 2, 4, P], F32R)
        hst = small("hst", [P, 2, T])
        assert c[0] <= size
        c[0] = o_phase
        hg = small("hg", [P, 4, 2, T])
        wt = small("wt", [P, T])
        assert c[0] <= size
        c[0] = o_after_ln
        sig = small("sig", [P, 2, T])
        yT = small("yT", [P, 2, T])
        yn = small("yn", [P, 2, TT, P])
        assert c[0] <= size

        ps = [ctx.enter_context(nc.psum_tensor(f"bank{i}", [P, T], F32)) for i in range(8)]
        ps_t, ps_s, ps_x, ps_o = ps[2:4], ps[4:6], ps[6], ps[7]

        raw_in = [sem("raw_in0"), sem("raw_in1")]
        hi_done = sem("hi_done")
        lo_done = sem("lo_done")
        blk_done = sem("blk_done")
        par_in = sem("par_in")
        x_in = [sem(f"x_in{i}") for i in range(4)]
        const_ok = sem("const_ok")
        x_pair = sem("x_pair")
        lam_prod = sem("lam_prod")
        lam_sum = sem("lam_sum")
        lam_exp = sem("lam_exp")
        setup_ok = sem("setup_ok")
        evac1 = sem("evac1")
        s_full = sem("s_full")
        s_free = sem("s_free")
        max_ok = sem("max_ok")
        exp_ok = sem("exp_ok")
        a_ok = sem("a_ok")
        vtr_full = sem("vtr_full")
        vn_ok = sem("vn_ok")
        t_full = sem("t_full")
        aT_ok = sem("aT_ok")
        o_full = sem("o_full")
        rms_ok = sem("rms_ok")
        on_ok = sem("on_ok")
        oT_full = sem("oT_full")
        oT_hi = sem("oT_hi")
        oT_lo = sem("oT_lo")
        sg_ok = sem("sg_ok")
        conv_ok = sem("conv_ok")
        gate_out = [sem(f"gate_out{i}") for i in range(2)]
        ln = [{n: sem(f"{n}{i}") for n in ("mean", "cent", "sqr", "sqr_used", "std_ok", "scaled", "affine", "hi_ok", "lo_ok")} for i in range(3)]
        evac2 = sem("evac2")
        gl_in = [sem("gl_in0"), sem("gl_in1")]
        mix_ok = sem("mix_ok")
        xr_in = [sem("xr_in0"), sem("xr_in1")]
        res_ok = sem("res_ok")
        keys_in = sem("keys_in")
        evac4 = sem("evac4")
        sc_full = sem("sc_full")
        sc_free = sem("sc_free")
        x1_out = sem("x1_out")
        soft_in = sem("soft_in")
        soft_exp = sem("soft_exp")
        picks_ok = sem("picks_ok")
        picks_full = sem("picks_full")
        picksT_ok = sem("picksT_ok")
        evac5 = sem("evac5")
        hot_ok = sem("hot_ok")
        g_full = sem("g_full")
        g_evac = sem("g_evac")
        gelu_out = [sem("gelu_out0"), sem("gelu_out1")]
        tile_out = sem("tile_out")
        x1_in = sem("x1_in")
        hg_in = [sem(f"hg_in{i}") for i in range(4)]
        w_ok = sem("w_ok")
        evac6 = sem("evac6")
        p_in = sem("p_in")
        p_ok = sem("p_ok")
        evac7 = sem("evac7")
        evac8 = sem("evac8")
        y_ok = sem("y_ok")
        yT_full = sem("yT_full")
        yn_ok = sem("yn_ok")
        out_done = [sem("out_done0"), sem("out_done1")]

        block = ctx.enter_context(nc.Block())

        @block.sync
        def _(sp):
            def load_unit(u, s):
                nxt = sp.snap(u + 2)
                sp.wait_ge(lo_done, 2 * u + 2)
                sp.dma_start(raw[:, s], ws[nxt]).then_inc(raw_in[s], 16)

            sp.dma_start(par[:], cpar).then_inc(par_in, 16)
            sp.dma_start(pv[:], pvec).then_inc(par_in, 16)
            sp.dma_start(lamv[:], lamT).then_inc(par_in, 16)
            sp.dma_start(raw[:, 0], ws[0]).then_inc(raw_in[0], 16)
            for q in range(4):
                sp.dma_start(xin[:, 4 * q:4 * q + 4], xT[:, 4 * q:4 * q + 4]).then_inc(x_in[q], 16)
            sp.dma_start(raw[:, 1], ws[1]).then_inc(raw_in[1], 16)

            with sp.Fori(0, (U1 + U1T) // 2) as i:
                for s in range(2):
                    load_unit(2 * i + s, s)

            def load_gates(j, s):
                j = sp.snap(j)
                sp.dma_start(gl[:, s, 0], gate_sp[j]).then_inc(gl_in[s], 16)
                sp.dma_start(gl[:, s, 1], gate_sp[j + KD]).then_inc(gl_in[s], 16)

            sp.wait_ge(ln[0]["lo_ok"], NH)
            sp.wait_ge(gate_out[0], 16 * (2 * NH + U1T // 2))
            sp.wait_ge(gate_out[1], 16 * (NH + U1T // 2))
            for s in range(2):
                load_gates(s, s)
            with sp.Fori(0, U2 // 2 - 1) as i:
                for s in range(2):
                    load_unit(2 * i + (B2 // 2 + s), s)
                    nxt = sp.snap(2 * i + s + 2)
                    sp.wait_ge(mix_ok, 2 * i + s + 1)
                    load_gates(nxt, s)
            for s in range(2):
                load_unit(B2 // 2 + U2 - 2 + s, s)

            def load_x(j, s):
                j = sp.snap(j)
                sp.dma_start(xr[:, s], xT[:, j]).then_inc(xr_in[s], 16)

            for s in range(2):
                load_x(s, s)
            sp.wait_ge(mix_ok, U2)
            sp.dma_start(keys[:], keysT).then_inc(keys_in, 16)
            with sp.Fori(0, U3 // 2 - 1) as i:
                for s in range(2):
                    load_unit(2 * i + (B3 // 2 + s), s)
                    nxt = sp.snap(2 * i + s + 2)
                    sp.wait_ge(res_ok, 2 * i + s + 1)
                    load_x(nxt, s)
            for s in range(2):
                load_unit(B3 // 2 + U3 - 2 + s, s)

            def spill_x1(q):
                sp.wait_ge(res_ok, KD + 4 * q + 4)
                sp.dma_start(x1_sp[:, 4 * q:4 * q + 4], res[:, 4 * q:4 * q + 4]).then_inc(x1_out, 16)

            for s in range(2):
                load_unit(B4 // 2 + s, s)
            for q in range(4):
                spill_x1(q)
            with sp.Fori(1, U4 // 2) as i:
                for s in range(2):
                    load_unit(2 * i + (B4 // 2 + s), s)

            def expert_loads(t, first, last):
                with sp.Fori(first, last) as i:
                    for s in range(2):
                        load_unit(t * 32 + i * 2 + (B5 // 2 + s), s)

            def tile_loads(t, start):
                expert_loads(t, 0, start + 9)
                sp.wait_ge(g_evac, t * 32 + (2 + 32))
                tt = sp.snap(t)
                for q in range(4):
                    sp.dma_start(route_sp[tt, :, q * 4096:(q + 1) * 4096],
                                 gst[:, q * 4096:(q + 1) * 4096]).then_inc(tile_out, 16)
                expert_loads(t, start + 9, 16)

            tile_loads(0, ROUTE0)
            with sp.Fori(1, TT) as t:
                tile_loads(t, 0)

            def load_hg(k, s):
                k = sp.snap(k)
                sp.dma_start(hg[:, s, 0], gelu_sp[k]).then_inc(hg_in[s], 16)
                kk = sp.snap(k * P)
                sp.dma_start(hg[:, s, 1].rearrange("p (a t) -> p a t", a=TT),
                             route_sp[:, :, bass.ds(kk, P)].rearrange("a p t -> p a t")).then_inc(hg_in[s], 16)

            sp.wait_ge(tile_out, 64 * TT)
            sp.wait_ge(x1_out, 64)
            for q in range(4):
                sp.dma_start(res[:, 4 * q:4 * q + 4], x1_sp[:, 4 * q:4 * q + 4]).then_inc(x1_in, 16)
            sp.wait_ge(blk_done, B6)
            for s in range(2):
                sp.wait_ge(gelu_out[s], 16 * (U5 // 2))
            sp.dma_start(hg[:, 3], pT).then_inc(p_in, 16)
            for k in range(3):
                load_hg(k, k)
            for k in range(3, 8):
                if k == 3:
                    sp.wait_ge(p_ok, 1)
                else:
                    sp.wait_ge(w_ok, k - 3)
                load_hg(k, k % 4)

            def group_loads(g, k):
                load_unit(g * 8 + (B6 // 2 + k), k % 2)
                nxt = sp.snap(g * 8 + (8 + k))
                sp.wait_ge(w_ok, g * 8 + (8 + k - 3))
                load_hg(nxt, k % 4)

            with sp.Fori(0, 15) as g:
                for k in range(8):
                    group_loads(g, k)
            for k in range(8):
                load_unit(B6 // 2 + 15 * 8 + k, k % 2)

            with sp.Fori(0, (U7 + U8) // 2 - 1) as i:
                for s in range(2):
                    load_unit(2 * i + (B7 // 2 + s), s)
            for s in range(2):
                sp.wait_ge(out_done[s], 16 * KD // 2)

        @block.gpsimd
        def _(pool):
            nc.gpsimd.memset(ones[:], 1.0)
            nc.gpsimd.memset(eps[:], EPS)
            nc.gpsimd.memset(ident[:], 0.0)
            nc.gpsimd.memset(glu[:, 0:W - 1], 0.0)
            nc.gpsimd.iota(iota[:], [[1, NK]], base=0, channel_multiplier=0,
                           allow_small_or_imprecise_dtypes=True)
            nc.gpsimd.iota(nd[:], [[1, T]], base=-(T - P), channel_multiplier=-1,
                           allow_small_or_imprecise_dtypes=True)
            pool.drain()
            nc.gpsimd.affine_select(out=ident[:], in_=ident[:], compare_op=ALU.not_equal, fill=1.0,
                                    base=0, pattern=[[-1, P]], channel_multiplier=1)
            nc.gpsimd.affine_select(out=nd[:], in_=nd[:], compare_op=ALU.is_ge, fill=-1e30,
                                    base=T - P, pattern=[[-1, T]], channel_multiplier=1)
            pool.drain().then_inc(const_ok, 1)

            with pool.Fori(0, NB // 4) as i:
                for s in range(4):
                    pool.wait_ge(hi_done, 4 * i + s + 1)
                    nc.gpsimd.tensor_tensor(wlo[:, s], raw[:, s // 2, s % 2], whi[:, s].bitcast(F32),
                                            ALU.subtract).then_inc(lo_done, 1)

        @block.tensor
        def _(pe):
            def three(ps_out, hi, lo, xh, xl, first, last):
                pe.matmul(ps_out, hi, xh, start=first, stop=False)
                pe.matmul(ps_out, hi, xl, start=False, stop=False)
                return pe.matmul(ps_out, lo, xh, start=False, stop=last)

            def one_block(b, s, bank, half, wait_x=None):
                pe.wait_ge(lo_done, b + 1)
                for k in range(8):
                    kk = 8 * half + k
                    if wait_x is not None:
                        pe.wait_ge(wait_x, kk + 1)
                    t = slice(k * P, (k + 1) * P)
                    mm = three(ps[bank][:], whi[:, s, t], wlo[:, s, t], ahi[:, kk], alo[:, kk],
                               kk == 0, kk == KD - 1)
                mm.then_inc(blk_done, 1)

            def norm_mean(i, n, src, first=0):
                for k in range(first, n):
                    mm = pe.matmul(ps_x[:], ones[:], src[:, k], start=(k == 0), stop=(k == n - 1))
                mm.then_inc(ln[i]["mean"], 1)

            def norm_var(i, n):
                for k in range(n):
                    pe.wait_ge(ln[i]["sqr"], k + 1)
                    mm = pe.matmul(ps_o[:], ones[:], sq[:, k % 2], start=(k == 0), stop=(k == n - 1))
                    mm.then_inc(ln[i]["sqr_used"], 1)

            pe.wait_ge(const_ok, 1)
            pe.wait_ge(lam_prod, 1)
            pe.matmul(ps_x[:, 0:2], ones[0:64, :], lamp[:], start=True, stop=True).then_inc(lam_sum, 1)

            def scores(h, b):
                if b == 0:
                    pe.wait_ge(evac1, 8 * h + 4)
                else:
                    pe.wait_ge(s_free, 4 * h + b)
                for m in range(2):
                    r = slice(64 * m, 64 * m + 64)
                    mm = pe.matmul(ps_s[m][:, 0:(b + 1) * P], qT[r, b * P:(b + 1) * P],
                                   kT[r, 0:(b + 1) * P], start=True, stop=True)
                mm.then_inc(s_full, 1)

            def turn_v(h):
                pe.wait_ge(evac1, 8 * h + 5)
                for k in range(TT):
                    mm = pe.transpose(ps_o[:, k * P:(k + 1) * P], vT[:, k * P:(k + 1) * P], ident[:])
                mm.then_inc(vtr_full, 1)

            def turn_a(h, b):
                pe.wait_ge(a_ok, 4 * h + b + 1)
                if b >= 2:
                    pe.wait_ge(aT_ok, 4 * h + b - 1)
                for k in range(b + 1):
                    mm = pe.transpose(ps_t[b % 2][:, k * P:(k + 1) * P], aN[:, k * P:(k + 1) * P], ident[:])
                mm.then_inc(t_full, 1)

            def weigh_v(h, b):
                if b == 0:
                    pe.wait_ge(vn_ok, h + 1)
                pe.wait_ge(aT_ok, 4 * h + b + 1)
                for k in range(b + 1):
                    mm = pe.matmul(ps_o[:, b * P:(b + 1) * P], aT[:, b % 2, k * P:(k + 1) * P],
                                   vn[:, k], start=(k == 0), stop=(k == b))
                if b == TT - 1:
                    mm.then_inc(o_full, 1)

            def turn_o(h):
                pe.wait_ge(on_ok, h + 1)
                for k in range(TT):
                    mm = pe.transpose(ps_x[:, k * P:(k + 1) * P], on[:, k * P:(k + 1) * P], ident[:])
                mm.then_inc(oT_full, 1)

            pe.wait_ge(setup_ok, 1)
            def head(h, first=False):
                for n in range(16):
                    if n % 2 == 0:
                        pe.wait_ge(evac1, 8 * h + n // 2 + 1)
                    one_block(16 * h + n, n % 4, n // 2 % 2, n % 2,
                              wait_x=x_pair if first and n < 2 else None)
                    if n == 2 and not first:
                        turn_o(h - 1)
                    if n == 4:
                        scores(h, 0)
                    if n == 6:
                        turn_v(h)
                        scores(h, 1)
                    if n == 7:
                        turn_a(h, 0)
                    if n == 8:
                        scores(h, 2)
                    if n == 9:
                        weigh_v(h, 0)
                        turn_a(h, 1)
                    if n == 10:
                        scores(h, 3)
                    if n == 11:
                        weigh_v(h, 1)
                        turn_a(h, 2)
                    if n == 12:
                        turn_a(h, 3)
                    if n == 13:
                        weigh_v(h, 2)
                        weigh_v(h, 3)

            head(0, first=True)
            with pe.Fori(1, NH) as h:
                head(h)
            for n in range(2 * U1T):
                if n % 2 == 0:
                    pe.wait_ge(evac1, U1 + n // 2 + 1)
                one_block(B1T + n, n % 4, n // 2 % 2, n % 2)
                if n == 1:
                    turn_o(NH - 1)
                if n == 3:
                    pe.wait_ge(conv_ok, NH)
                    pe.wait_ge(oT_hi, NH)
                    norm_mean(0, NH, conv)
                if n == 5:
                    norm_var(0, NH)

            def branch_unit(j, s, wait_x=False):
                for half, (xh, xl) in enumerate(((swhi, swlo), (oThi, oTlo))):
                    pe.wait_ge(lo_done, 2 * j + (B2 + half + 1))
                    for k in range(8):
                        if wait_x and half == 0:
                            pe.wait_ge(ln[0]["lo_ok"], k + 1)
                        t = slice(k * P, (k + 1) * P)
                        w = 2 * s + half
                        mm = three(ps[w][:], whi[:, w, t], wlo[:, w, t], xh[:, k], xl[:, k], k == 0, k == 7)
                    mm.then_inc(blk_done, 1)

            pe.wait_ge(evac1, 2 + U1 + U1T)
            pe.wait_ge(oT_lo, NH)
            for s in range(2):
                branch_unit(s, s, wait_x=(s == 0))
            with pe.Fori(1, U2 // 2) as i:
                for s in range(2):
                    pe.wait_ge(evac2, 2 * i + s - 1)
                    branch_unit(2 * i + s, s)

            def out_unit(j, s, first=False):
                for half in range(2):
                    one_block(2 * j + (B3 + half), 2 * s + half, s, half,
                              wait_x=mix_ok if first and s == 0 else None)
                    if half == 0 and not (first and s == 0):
                        pe.wait_ge(res_ok, j)
                        pe.matmul(ps_x[:], ones[:], res[:, j - 1], start=(first and s == 1), stop=False)

            pe.wait_ge(evac2, U2)
            out_unit(0, 0, first=True)
            out_unit(1, 1, first=True)
            with pe.Fori(1, U3 // 2) as i:
                for s in range(2):
                    out_unit(2 * i + s, s)
            pe.wait_ge(res_ok, KD)
            norm_mean(1, KD, res, first=KD - 1)
            norm_var(1, KD)

            def key_scores(hc, s):
                pe.wait_ge(evac4, hc + 1)
                for a in range(TT):
                    mm = pe.matmul(ps_s[s][:, a * P:(a + 1) * P], qs[:, s, a * P:(a + 1) * P],
                                   keys[:, hc], start=True, stop=True)
                mm.then_inc(sc_full, 1)

            def query_pair(i, first=False):
                for s in range(2):
                    for half in range(2):
                        one_block(4 * i + (B4 + 2 * s + half), 2 * s + half, s, half,
                                  wait_x=ln[1]["lo_ok"] if first and s == 0 else None)
                        if half == 0 and not (first and s == 0):
                            pe.wait_ge(sc_free, 2 * i + s)
                            key_scores(2 * i + (s - 1), 1 - s)

            pe.wait_ge(keys_in, 16)
            query_pair(0, first=True)
            with pe.Fori(1, PH) as i:
                query_pair(i)

            def turn_picks():
                pe.wait_ge(picks_ok, 1)
                for dst, src in ((ps_s[0], gn), (ps_s[1], i1n), (ps_x, i2n)):
                    for a in range(TT):
                        mm = pe.transpose(dst[:, a * P:(a + 1) * P],
                                          src[:, a].rearrange("p h k -> p (h k)"), ident[:])
                mm.then_inc(picks_full, 1)

            def route(g, s):
                pe.wait_ge(hot_ok, g + 1)
                pe.wait_ge(g_evac, g + 1)
                for k in range(4):
                    o = ps_t[s][:, k * P:(k + 1) * P]
                    pe.matmul(o, hot1[:, s, k], hot2h[:, s, k], start=True, stop=False)
                    mm = pe.matmul(o, hot1[:, s, k], hot2l[:, s, k], start=False, stop=True)
                mm.then_inc(g_full, 1)

            def expert_steps(t, first, last, route_from=None):
                with pe.Fori(first, last) as i:
                    for s in range(2):
                        pe.wait_ge(evac5, t * 32 + i * 2 + (s + 1))
                        for half in range(2):
                            one_block(t * 64 + i * 4 + (B5 + 2 * s + half), 2 * s + half, s, half)
                            if route_from is not None:
                                route(t * 32 + i * 4 + (2 * s + half - 4 * route_from), half)

            pe.wait_ge(evac4, U4)
            pe.wait_ge(sc_free, U4)
            key_scores(U4 - 1, 1)
            expert_steps(0, 0, ROUTE0)
            pe.wait_ge(sc_free, U4 + 2)
            turn_picks()
            expert_steps(0, ROUTE0, ROUTE0 + 8, ROUTE0)
            expert_steps(0, ROUTE0 + 8, 16)
            with pe.Fori(1, TT) as t:
                expert_steps(t, 0, 8, 0)
                expert_steps(t, 8, 16)

            def value_group(g, q):
                pe.wait_ge(w_ok, g * 8 + 8)
                for u in range(8):
                    pe.wait_ge(evac6, g * 8 + (u + 1))
                    for half in range(2):
                        b, s = g * 16 + (B6 + 2 * u + half), 2 * (u % 2) + half
                        pe.wait_ge(lo_done, b + 1)
                        for k in range(8):
                            t = slice(k * P, (k + 1) * P)
                            mm = three(ps[s][:], whi[:, s, t], wlo[:, s, t],
                                       xwhi[q][:, k], xwlo[q][:, k], k == 0, k == 7)
                        mm.then_inc(blk_done, 1)

            pe.wait_ge(evac5, 2 + U5)
            pe.wait_ge(g_evac, 2 + T // 4)
            with pe.Fori(0, 8) as i:
                for q in range(2):
                    value_group(2 * i + q, q)

            pe.wait_ge(evac6, 2 + U6)
            for n in range(4):
                pe.wait_ge(lo_done, B7 + n + 1)
                if n >= 2:
                    pe.wait_ge(evac7, 4 * (n - 1))
                for j in range(4):
                    for k in range(2):
                        t = slice((2 * j + k) * P, (2 * j + k + 1) * P)
                        mm = three(ps[4 * (n % 2) + j][:], whi[:, n, t], wlo[:, n, t],
                                   ahi[:, 8 + k], alo[:, 8 + k], k == 0, k == 1)
                mm.then_inc(blk_done, 1)
            pe.wait_ge(evac7, KD)
            norm_mean(2, KD, res)
            norm_var(2, KD)

            def turn_y(m, s):
                pe.wait_ge(y_ok, m + 1)
                pe.wait_ge(yn_ok, m + 1)
                for a in range(TT):
                    mm = pe.transpose(ps_t[s][:, a * P:(a + 1) * P], yT[:, s, a * P:(a + 1) * P], ident[:])
                mm.then_inc(yT_full, 1)

            def ple_pair(i, first=False):
                for s in range(2):
                    if not first:
                        pe.wait_ge(evac8, 2 * i + (s - 1))
                    for half in range(2):
                        one_block(4 * i + (B8 + 2 * s + half), 2 * s + half, s, half,
                                  wait_x=ln[2]["lo_ok"] if first and s == 0 else None)
                        if half == 0 and not (first and s == 0):
                            turn_y(2 * i + (s - 1), 1 - s)

            ple_pair(0, first=True)
            with pe.Fori(1, U8 // 2) as i:
                ple_pair(i)
            turn_y(U8 - 1, 1)

        @block.scalar
        def _(act):
            def hi_part(b, s, unit=None):
                nxt = b + AHEAD
                act.wait_ge(blk_done, b + 1)
                act.wait_ge(raw_in[s // 2], unit)
                act.activation(whi[:, s], raw[:, s // 2, s % 2], ACT.Copy).then_inc(hi_done, 1)

            def step(b, s):
                hi_part(b, s, (b - s) * 4 + 32)

            def norm_squares(i, n, src):
                for k in range(n):
                    act.wait_ge(ln[i]["cent"], k + 1)
                    if k >= 2:
                        act.wait_ge(ln[i]["sqr_used"], k - 1)
                    act.activation(sq[:, k % 2], src[:, k], ACT.Square).then_inc(ln[i]["sqr"], 1)
                act.wait_ge(ln[i]["sqr_used"], n)
                act.activation(std[:], ps_o[:], ACT.Sqrt, bias=eps[:], scale=1.0 / (n * P)
                               ).then_inc(ln[i]["std_ok"], 1)

            def norm_affine(i, n, dst, hi, func, gain, bias):
                for k in range(n):
                    act.wait_ge(ln[i]["scaled"], k + 1)
                    act.activation(dst[:, k], nrm[:, k % 2], func, bias=bias(k), scale=gain(k)
                                   ).then_inc(ln[i]["affine"], 1)
                    act.drain()
                    act.activation(hi[:, k], dst[:, k], ACT.Copy).then_inc(ln[i]["hi_ok"], 1)

            act.sem_inc(evac1, 2)
            act.sem_inc(evac5, 2)
            act.sem_inc(g_evac, 2)
            act.sem_inc(yn_ok, 2)
            for s in range(4):
                act.wait_ge(raw_in[s // 2], 16)
                act.activation(whi[:, s], raw[:, s // 2, s % 2], ACT.Copy).then_inc(hi_done, 1)
            act.wait_ge(lam_sum, 1)
            act.activation(lame[:], ps_x[:, 0:2], ACT.Exp).then_inc(lam_exp, 1)
            act.wait_ge(setup_ok, 1)

            def softmax_exp(h, b):
                act.wait_ge(max_ok, 4 * h + b + 1)
                n = (b + 1) * P
                for m in range(2):
                    e = act.activation(sc[:, m, 0:n], sc[:, m, 0:n], ACT.Exp, bias=nmx[:, m:m + 1],
                                       accum_out=sums[:, m:m + 1])
                act.drain().then_inc(exp_ok, 1)

            def take_aT(h, b):
                act.wait_ge(t_full, 4 * h + b + 1)
                n = (b + 1) * P
                act.copy(aT[:, b % 2, 0:n], ps_t[b % 2][:, 0:n]).then_inc(aT_ok, 1)

            def take_gate(g, bank, slot):
                act.activation(gout[:, slot], ps[bank][:], ACT.Sigmoid, bias=pv[:, bass.ds(g + V_BG, 1)]
                               ).then_inc(evac1, 1)
                act.drain()
                act.dma_start(gate_sp[g], gout[:, slot]).then_inc(gate_out[slot], 16)

            def take_o(h):
                act.wait_ge(oT_full, h + 1)
                act.activation(oTf[:], ps_x[:], ACT.Copy, scale=sub8[:])
                act.drain()
                act.activation(oThi[:, h], oTf[:], ACT.Copy).then_inc(oT_hi, 1)

            def head(h, first=False):
                for n in range(16):
                    step(16 * h + n, n % 4)
                    if n == 3 and not first:
                        take_o(h - 1)
                    if n == 1:
                        act.mul(qT[:], ps[0][:], 0.125).then_inc(evac1, 1)
                    if n == 3:
                        act.copy(kT[:], ps[1][:]).then_inc(evac1, 1)
                    if n == 5:
                        act.copy(vT[:], ps[0][:]).then_inc(evac1, 1)
                        softmax_exp(h, 0)
                    if n == 6:
                        act.wait_ge(vtr_full, h + 1)
                        act.copy(vn[:].rearrange("p a b -> p (a b)"), ps_o[:]).then_inc(vn_ok, 1)
                    if n == 7:
                        act.copy(glu[:, W - 1:], ps[1][:]).then_inc(evac1, 1)
                        softmax_exp(h, 1)
                    if n == 8:
                        take_aT(h, 0)
                    if n == 9:
                        act.activation(sg[:], ps[0][:], ACT.Sigmoid).then_inc(evac1, 1)
                        act.drain().then_inc(sg_ok, 1)
                        softmax_exp(h, 2)
                    if n == 10:
                        take_aT(h, 1)
                    if n == 11:
                        softmax_exp(h, 3)
                        take_gate(3 * h, 1, 0)
                    if n == 12:
                        take_aT(h, 2)
                        take_aT(h, 3)
                    if n == 13:
                        take_gate(3 * h + 1, 0, 1)
                    if n == 14:
                        act.wait_ge(o_full, h + 1)
                        for b in range(TT):
                            if b:
                                act.drain()
                            act.activation(junk[:], ps_o[:, b * P:(b + 1) * P],
                                           ACT.Square, accum_out=ssq[:, b:b + 1])
                        act.drain()
                        act.activation(rms[:], ssq[:], ACT.Sqrt, bias=eps[:], scale=1.0 / P
                                       ).then_inc(rms_ok, 1)
                    if n == 15:
                        act.wait_ge(gate_out[0], 32 * h + 16)
                        take_gate(3 * h + 2, 1, 0)
                        act.wait_ge(gate_out[0], 32 * h + 32)
                        act.wait_ge(gate_out[1], 16 * h + 16)

            head(0, first=True)
            with act.Fori(1, NH) as h:
                head(h)
            for n in range(2 * U1T):
                step(B1T + n, n % 4)
                if n % 2 == 1:
                    u = n // 2
                    if u >= 2:
                        act.wait_ge(gate_out[u % 2], (2 - u % 2) * 16 * NH + 16 * (u // 2))
                    take_gate(FIRST_GATE_TAIL + u, u % 2, u % 2)
                if n == 2:
                    take_o(NH - 1)
                if n == 4:
                    norm_squares(0, NH, conv)
                if n == 8:
                    norm_affine(0, NH, conv, swhi, ACT.Silu,
                                lambda k: par[:, k, C_LNG:C_LNG + 1], lambda k: par[:, k, C_LNB:C_LNB + 1])

            with act.Fori(0, (U2 + U3) // 2) as i:
                for s in range(4):
                    step(4 * i + (B2 + s), s)
            norm_squares(1, KD, res)
            norm_affine(1, KD, res, ahi, ACT.Identity,
                        lambda k: pv[:, V_LN1G + k:V_LN1G + k + 1], lambda k: pv[:, V_LN1B + k:V_LN1B + k + 1])

            with act.Fori(0, PH) as i:
                for s in range(4):
                    step(4 * i + (B4 + s), s)
                    if s % 2 == 1:
                        act.copy(qs[:, s // 2], ps[s // 2][:]).then_inc(evac4, 1)

            def take_group(t, g, tok, s):
                act.wait_ge(g_full, g + 1)
                act.copy(gst[:].rearrange("p (k t) -> p t k", t=P)[:, bass.ds(tok, 4), :],
                         ps_t[s][:].rearrange("p (t k) -> p t k", t=4)).then_inc(g_evac, 1)

            def expert_step(t, i, first=False, route_from=None):
                for s in range(4):
                    step(t * 64 + i * 4 + (B5 + s), s)
                    if s % 2 == 1:
                        u = s // 2
                        if not (first and u == 0):
                            act.wait_ge(gelu_out[1 - u], t * 256 + i * 16 + 16 * u)
                        act.activation(hst[:, u], ps[u][:], ACT.Gelu_apprx_tanh).then_inc(evac5, 1)
                        act.drain()
                        act.dma_start(gelu_sp[t * 32 + i * 2 + u], hst[:, u]).then_inc(gelu_out[u], 16)
                    if route_from is not None:
                        take_group(t, t * 32 + i * 4 + (s - 4 * route_from),
                                   i * 16 + (4 * s - 16 * route_from), s % 2)

            def expert_steps(t, first, last, route_from=None):
                with act.Fori(first, last) as i:
                    expert_step(t, i, route_from=route_from)

            expert_step(0, 0, first=True)
            expert_steps(0, 1, ROUTE0)
            act.wait_ge(soft_in, 1)
            act.activation(gn[:], gn[:], ACT.Exp).then_inc(soft_exp, 1)
            act.wait_ge(x1_out, 64)
            expert_steps(0, ROUTE0, ROUTE0 + 8, ROUTE0)
            expert_steps(0, ROUTE0 + 8, 16)
            with act.Fori(1, TT) as t:
                act.wait_ge(tile_out, t * 64)
                expert_steps(t, 0, 8, 0)
                expert_steps(t, 8, 16)

            with act.Fori(0, U6 // 2) as i:
                for s in range(4):
                    step(4 * i + (B6 + s), s)

            for n in range(4):
                step(B7 + n, n)
                for j in range(4):
                    act.copy(eT[:, 4 * n + j], ps[4 * (n % 2) + j][:]).then_inc(evac7, 1)
            norm_squares(2, KD, res)
            norm_affine(2, KD, res, ahi, ACT.Identity,
                        lambda k: pv[:, V_LN2G + k:V_LN2G + k + 1], lambda k: pv[:, V_LN2B + k:V_LN2B + k + 1])

            def take_y(m, s, first=False):
                act.wait_ge(yT_full, m + 1)
                if not first:
                    act.wait_ge(out_done[1 - s], (m + s) * 8)
                act.copy(yn[:, s].rearrange("p a b -> p (a b)"), ps_t[s][:]).then_inc(yn_ok, 1)
                act.drain()
                act.dma_start(out2.rearrange("(a p) (j d) -> j p a d", p=P, d=P)[m], yn[:, s]
                              ).then_inc(out_done[s], 16)

            def ple_pair(i, first=False, last=False):
                for s in range(4):
                    b = 4 * i + (B8 + s)
                    if last:
                        act.wait_ge(blk_done, b + 1)
                    else:
                        step(b, s)
                    if s % 2 == 0 and not (first and s == 0):
                        m, ms = 2 * i + (s // 2 - 1), 1 - s // 2
                        take_y(m, ms, first and s == 2)
                    if s % 2 == 1:
                        u = s // 2
                        act.activation(sig[:, u], ps[u][:], ACT.Sigmoid,
                                       bias=pv[:, bass.ds(2 * i + (V_PLEB + u), 1)]).then_inc(evac8, 1)

            ple_pair(0, first=True)
            with act.Fori(1, U8 // 2 - 1) as i:
                ple_pair(i)
            ple_pair(U8 // 2 - 1, last=True)
            take_y(U8 - 1, 1)

        @block.vector
        def _(dve):
            dve.sem_inc(sc_free, 2)
            dve.sem_inc(evac6, 2)
            dve.wait_ge(par_in, 48)
            dve.tensor_tensor(lamp[:], lamv[:, 0:4:2], lamv[:, 1:4:2], ALU.mult).then_inc(lam_prod, 1)
            dve.tensor_scalar(sub8[:], pv[:, V_SUB:V_SUB + 1], 1.0 - LAM0, None, ALU.mult)
            dve.wait_ge(lam_exp, 1)
            dve.tensor_tensor(nlam[:], lame[:, 1:2], lame[:, 0:1], ALU.subtract)
            dve.drain()
            dve.tensor_scalar(nlam[:], nlam[:], -LAM0, None, ALU.add)
            dve.wait_ge(const_ok, 1)
            dve.drain().then_inc(setup_ok, 1)
            for q in range(4):
                k = slice(4 * q, 4 * q + 4)
                dve.wait_ge(x_in[q], 16)
                dve.tensor_copy(ahi[:, k], xin[:, k])
                dve.drain()
                dve.tensor_tensor(alo[:, k], xin[:, k], ahi[:, k].bitcast(F32), ALU.subtract
                                  ).then_inc(x_pair, 4)

            def attention_weights(h, b):
                n = (b + 1) * P
                dve.drain()
                dve.wait_ge(s_full, 4 * h + b + 1)
                for m in range(2):
                    st = dve.scalar_tensor_tensor(sc[:, m, 0:n], nd[:, T - n:], cur[:, C_SLOPE:C_SLOPE + 1],
                                                  ps_s[m][:, 0:n], ALU.mult, ALU.add)
                st.then_inc(s_free, 1)
                dve.drain()
                dve.tensor_reduce(nmx[:], sc[:, :, 0:n], AX.X, ALU.max, negate=True).then_inc(max_ok, 1)
                dve.wait_ge(exp_ok, 4 * h + b + 1)
                dve.reciprocal(rcp[:], sums[:])
                dve.drain()
                dve.tensor_tensor(rl[:], rcp[:, 1:2], nlam[:], ALU.mult)
                dve.drain()
                dve.tensor_scalar(sc[:, 1, 0:n], sc[:, 1, 0:n], rl[:], None, ALU.mult)
                dve.drain()
                if b >= 1:
                    dve.wait_ge(t_full, 4 * h + b)
                dve.scalar_tensor_tensor(aN[:, 0:n], sc[:, 0, 0:n], rcp[:, 0:1], sc[:, 1, 0:n],
                                         ALU.mult, ALU.add).then_inc(a_ok, 1)

            def o_low(h):
                dve.wait_ge(oT_hi, h + 1)
                dve.tensor_tensor(oTlo[:, h], oTf[:], oThi[:, h].bitcast(F32), ALU.subtract
                                  ).then_inc(oT_lo, 1)

            def head(h, first=False):
                dve.drain()
                dve.tensor_copy(cur[:], par[:, h])
                dve.drain()
                for b in range(TT):
                    attention_weights(h, b)
                    if b == 0 and not first:
                        o_low(h - 1)
                dve.wait_ge(sg_ok, h + 1)
                dve.tensor_tensor(glu[:, W - 1:], glu[:, W - 1:], sg[:], ALU.mult)
                dve.drain()
                dve.tensor_scalar(acc, glu[:, 0:T], cur[:, 0:1], cur[:, C_BIAS:C_BIAS + 1],
                                  ALU.mult, ALU.add)
                for w in range(1, W):
                    dve.drain()
                    dst = acc if w < W - 1 else conv[:, h]
                    cv = dve.scalar_tensor_tensor(dst, glu[:, w:w + T], cur[:, w:w + 1], acc,
                                                  ALU.mult, ALU.add)
                cv.then_inc(conv_ok, 1)
                dve.wait_ge(rms_ok, h + 1)
                dve.reciprocal(rrms[:], rms[:])
                dve.drain()
                dve.tensor_tensor(on[:].rearrange("p (a b) -> p a b", a=TT),
                                  ps_o[:].rearrange("p (a b) -> p a b", a=TT),
                                  rrms[:].unsqueeze(2).broadcast_to((P, TT, P)), ALU.mult
                                  ).then_inc(on_ok, 1)

            head(0, first=True)
            with dve.Fori(1, NH) as h:
                head(h)
            o_low(NH - 1)

            def norm(i, n, src, after):
                dve.drain()
                dve.wait_ge(ln[i]["mean"], 1)
                for k in range(n):
                    dve.scalar_tensor_tensor(src[:, k], ps_x[:], -1.0 / (n * P), src[:, k],
                                             ALU.mult, ALU.add).then_inc(ln[i]["cent"], 1)
                dve.wait_ge(ln[i]["std_ok"], 1)
                dve.reciprocal(rstd[:], std[:])
                dve.drain()
                for k in range(n + 1):
                    if k < n:
                        if k >= 2:
                            dve.wait_ge(ln[i]["affine"], k - 1)
                        dve.tensor_tensor(nrm[:, k % 2], src[:, k], rstd[:], ALU.mult
                                          ).then_inc(ln[i]["scaled"], 1)
                    if k >= 1:
                        dve.wait_ge(ln[i]["hi_ok"], k)
                        after(k - 1)

            def after_conv(k):
                dve.tensor_tensor(swlo[:, k], conv[:, k], swhi[:, k].bitcast(F32), ALU.subtract
                                  ).then_inc(ln[0]["lo_ok"], 1)

            norm(0, NH, conv, after_conv)

            with dve.Fori(0, U2 // 2) as i:
                for s in range(2):
                    dve.wait_ge(gl_in[s], 32 * i + 32)
                    dve.wait_ge(blk_done, 4 * i + (B2 + 2 * s + 2))
                    dve.tensor_tensor(gl[:, s, 0], gl[:, s, 0], ps[2 * s][:], ALU.mult)
                    dve.tensor_tensor(gl[:, s, 1], gl[:, s, 1], ps[2 * s + 1][:], ALU.mult).then_inc(evac2, 1)
                    dve.drain()
                    dve.tensor_tensor(mt[:], gl[:, s, 0], gl[:, s, 1], ALU.add)
                    dve.drain()
                    dve.tensor_copy(ahi[:, 2 * i + s], mt[:])
                    dve.drain()
                    dve.tensor_tensor(alo[:, 2 * i + s], mt[:], ahi[:, 2 * i + s].bitcast(F32),
                                      ALU.subtract).then_inc(mix_ok, 1)

            with dve.Fori(0, U3 // 2) as i:
                for s in range(2):
                    dve.wait_ge(xr_in[s], 16 * i + 16)
                    dve.wait_ge(blk_done, 4 * i + (B3 + 2 * s + 2))
                    dve.scalar_tensor_tensor(res[:, 2 * i + s], xr[:, s], ALPHA, ps[s][:],
                                             ALU.mult, ALU.add).then_inc(res_ok, 1)

            def after_ln1(k):
                dve.tensor_tensor(alo[:, k], res[:, k], ahi[:, k].bitcast(F32), ALU.subtract
                                  ).then_inc(ln[1]["lo_ok"], 1)
                dve.drain()
                dve.tensor_scalar(res[:, k], res[:, k], ALPHA, None, ALU.mult).then_inc(res_ok, 1)

            norm(1, KD, res, after_ln1)

            def best16(vals, idx, a, b):
                for t in range(TT):
                    dve.max(vals[:, t, 0:8], a[:, t])
                dve.drain()
                for t in range(TT):
                    dve.max_index(idx[:, t, 0:8], vals[:, t, 0:8], a[:, t])
                    dve.match_replace(b[:, t], vals[:, t, 0:8], a[:, t], -3e38)
                dve.drain()
                for t in range(TT):
                    dve.max(vals[:, t, 8:16], b[:, t])
                dve.drain()
                for t in range(TT):
                    dve.max_index(idx[:, t, 8:16], vals[:, t, 8:16], b[:, t])
                dve.drain()

            with dve.Fori(0, PH) as h:
                for cc in range(2):
                    dve.wait_ge(sc_full, 2 * h + cc + 1)
                    dve.tensor_copy(s4[:].rearrange("p a k -> p (a k)"), ps_s[cc][:]).then_inc(sc_free, 1)
                    dve.drain()
                    best16(top[:, cc], topi[:, cc], s4, s4b)
                dve.tensor_copy(k1f[:, :, h], topi[:, 0])
                dve.tensor_copy(k2f[:, :, h], topi[:, 1])
                dve.tensor_tensor(cand[:].rearrange("p t (a b) -> p t a b", a=TOPK),
                                  top[:, 0].unsqueeze(3).broadcast_to((P, TT, TOPK, TOPK)),
                                  top[:, 1].unsqueeze(2).broadcast_to((P, TT, TOPK, TOPK)), ALU.add)
                dve.drain()
                best16(bnow, pnow, cand, cand2)
                dve.tensor_copy(best[:, :, h], bnow[:])
                dve.tensor_copy(bpos[:, :, h], pnow[:])
            dve.drain()

            with dve.Fori(0, PH) as h:
                dve.tensor_copy(pnow[:], bpos[:, :, h])
                dve.tensor_copy(know[:, 0], k1f[:, :, h])
                dve.tensor_copy(know[:, 1], k2f[:, :, h])
                dve.drain()
                dve.tensor_scalar(pab[:, 0], pnow[:], 4, None, ALU.logical_shift_right)
                dve.tensor_scalar(pab[:, 1], pnow[:], 15, None, ALU.bitwise_and)
                dve.drain()
                dve.tensor_copy(pabf[:], pab[:])
                dve.drain()
                for cc, dst in ((0, i1n), (1, i2n)):
                    dve.tensor_tensor(hot[:], pabf[:, cc].unsqueeze(3).broadcast_to((P, TT, TOPK, TOPK)),
                                      iota[:, 0:TOPK].unsqueeze(1).unsqueeze(1).broadcast_to((P, TT, TOPK, TOPK)),
                                      ALU.is_equal)
                    dve.drain()
                    dve.tensor_tensor(hot[:], hot[:],
                                      know[:, cc].unsqueeze(2).broadcast_to((P, TT, TOPK, TOPK)), ALU.mult)
                    dve.drain()
                    dve.tensor_reduce(pick[:], hot[:], AX.X, ALU.add)
                    dve.drain()
                    dve.tensor_copy(dst[:, :, h], pick[:])
            dve.drain()
            rows = best[:].rearrange("p t h k -> p (t h) k")
            grows = gn[:].rearrange("p t h k -> p (t h) k")
            dve.tensor_tensor(grows, rows, rows[:, :, 0:1].broadcast_to((P, TT * PH, TOPK)), ALU.subtract
                              ).then_inc(soft_in, 1)
            dve.wait_ge(soft_exp, 1)
            dve.tensor_reduce(gsum[:], grows, AX.X, ALU.add)
            dve.drain()
            dve.reciprocal(grcp[:], gsum[:])
            dve.drain()
            dve.tensor_tensor(grows, grows, grcp[:].unsqueeze(2).broadcast_to((P, TT * PH, TOPK)), ALU.mult
                              ).then_inc(picks_ok, 1)
            dve.wait_ge(picks_full, 1)
            dve.tensor_copy(ghi[:], ps_s[0][:])
            dve.tensor_copy(i1T[:], ps_s[1][:])
            dve.tensor_copy(i2T[:], ps_x[:])
            dve.drain()
            dve.tensor_tensor(glo[:], ps_s[0][:], ghi[:].bitcast(F32), ALU.subtract)
            dve.drain()

            def one_hots(g, s):
                for k in range(4):
                    tok = bass.ds(4 * g + k, 1)
                    dve.tensor_scalar(hot1[:, s, k], iota[:], i1T[:, tok], None, ALU.is_equal)
                    dve.tensor_scalar(hot2h[:, s, k], iota[:], i2T[:, tok], ghi[:, tok].bitcast(F32),
                                      ALU.is_equal, ALU.mult)
                    oh = dve.tensor_scalar(hot2l[:, s, k], iota[:], i2T[:, tok], glo[:, tok].bitcast(F32),
                                           ALU.is_equal, ALU.mult)
                oh.then_inc(hot_ok, 1)

            for s in range(2):
                one_hots(s, s)
            with dve.Fori(1, T // 8) as i:
                for s in range(2):
                    dve.wait_ge(g_full, 2 * i + (s - 1))
                    one_hots(2 * i + s, s)

            def expert_weights(g, k, q):
                s = k % 4
                dve.drain()
                dve.wait_ge(hg_in[s], g * 64 + 32 * (k // 4 + 1))
                dve.tensor_tensor(wt[:], hg[:, s, 0], hg[:, s, 1], ALU.mult)
                dve.drain()
                dve.tensor_copy(xwhi[q][:, k], wt[:])
                dve.drain()
                dve.tensor_tensor(xwlo[q][:, k], wt[:], xwhi[q][:, k].bitcast(F32), ALU.subtract
                                  ).then_inc(w_ok, 1)

            dve.wait_ge(p_in, 16)
            dve.tensor_copy(ahi[:, 8:10], hg[:, 3])
            dve.drain()
            dve.tensor_tensor(alo[:, 8:10], hg[:, 3], ahi[:, 8:10].bitcast(F32), ALU.subtract
                              ).then_inc(p_ok, 1)
            for k in range(8):
                expert_weights(0, k, 0)
            dve.wait_ge(x1_in, 64)

            def add_values(g, q, last=False):
                for u in range(8):
                    if not last:
                        expert_weights(g + 1, u, 1 - q)
                    dve.wait_ge(blk_done, g * 16 + (B6 + 2 * u + 2))
                    for n in range(2):
                        ad = dve.tensor_tensor(res[:, 2 * u + n], res[:, 2 * u + n],
                                               ps[2 * (u % 2) + n][:], ALU.add)
                    ad.then_inc(evac6, 1)

            with dve.Fori(0, 7) as i:
                for q in range(2):
                    add_values(2 * i + q, q)
            add_values(14, 0)
            add_values(15, 1, last=True)

            def after_ln2(k):
                dve.tensor_tensor(alo[:, k], res[:, k], ahi[:, k].bitcast(F32), ALU.subtract
                                  ).then_inc(ln[2]["lo_ok"], 1)

            norm(2, KD, res, after_ln2)

            with dve.Fori(0, U8 // 2) as i:
                for s in range(2):
                    dve.wait_ge(evac8, 2 * i + s + 1)
                    dve.tensor_tensor(sig[:, s], sig[:, s], eT[:, 2 * i + s], ALU.mult)
                    dve.drain()
                    dve.tensor_tensor(yT[:, s], sig[:, s], res[:, 2 * i + s], ALU.add).then_inc(y_ok, 1)


def kernel(**inputs):
    import numpy as np
    import concourse.bacc as bacc
    from concourse.bass_utils import run_bass_kernel_spmd

    a = {k: np.asarray(v) for k, v in inputs.items()}

    def units(w):
        return w.reshape(2, 8, P, -1, P).transpose(3, 2, 0, 1, 4).reshape(-1, P, 2, 1024)

    win = units(a["w_in"][0])
    conv_v, conv_g = win[0:8], win[8:16]
    q, k, v, gates = win[16:24], win[24:32], win[32:40], win[40:72]
    heads = [np.concatenate([q[h:h + 1], k[h:h + 1], v[h:h + 1], conv_v[h:h + 1], conv_g[h:h + 1],
                             gates[3 * h:3 * h + 3]]) for h in range(NH)]
    branch = np.stack([a[n][0].reshape(8, P, KD, P).transpose(2, 1, 0, 3).reshape(KD, P, 1024)
                       for n in ("conv_w_out", "attn_w_o")], axis=2)
    u = a["peer_u"][0].reshape(NK, NK, 2, 8, P).transpose(1, 4, 2, 3, 0).reshape(-1, P, 2, 1024)
    vv = a["peer_v"][0].reshape(NK, 16, 8, 8, 2, P).transpose(1, 3, 0, 4, 2, 5).reshape(-1, P, 2, 1024)
    wp = a["ple_w_proj"][0].reshape(2, P, 2, 2, 4, P).transpose(2, 1, 3, 4, 0, 5).reshape(-1, P, 2, 1024)
    ws = np.concatenate(heads + [gates[FIRST_GATE_TAIL:], branch, units(a["w_out"][0]),
                                 units(a["peer_w_q"][0]), u, vv, wp, units(a["ple_w_gate"][0])])
    assert ws.shape == (NU, P, 2, 1024)
    slopes = 2.0 ** (-8.0 * np.arange(1, NH + 1) / NH)

    def chunks(x):
        return x.reshape(-1, P).T

    cols = [a["conv_dw_w"][0, :, 0].reshape(W, NH, P).transpose(2, 1, 0)]
    cols += [chunks(a[n][0])[:, :, None] for n in ("conv_dw_b", "conv_ln_g", "conv_ln_b")]
    cols.append(np.broadcast_to(slopes.astype(np.float32)[None, :, None], (P, NH, 1)))
    cols.append(np.zeros((P, NH, NCPAR - C_SLOPE - 1), np.float32))
    arrays = {
        "ws": ws,
        "xT": a["x"][0].T.reshape(KD, P, T).transpose(1, 0, 2),
        "pT": a["p"][0, 0].T.reshape(2, P, T).transpose(1, 0, 2),
        "cpar": np.concatenate(cols, axis=2),
        "pvec": np.concatenate([chunks(a[n][0]) for n in ("ln1_g", "ln1_b", "ln2_g", "ln2_b", "ple_b_gate",
                                                          "b_gate", "attn_subln_g")], axis=1),
        "lamT": np.stack([a["attn_lambda_" + n][0] for n in ("q1", "k1", "q2", "k2")], axis=1),
        "keysT": a["peer_sub_keys"][0].reshape(2 * PH, NK, P).transpose(2, 0, 1),
    }
    arrays = {n: np.ascontiguousarray(x) for n, x in arrays.items()}
    nc = bacc.Bacc("TRN2", target_bir_lowering=False, num_devices=1)
    args = [nc.dram_tensor(n, x.shape, F32, kind="ExternalInput").ap() for n, x in arrays.items()]
    args.append(nc.dram_tensor("y", (1, T, D), F32, kind="ExternalOutput").ap())
    build(nc, *args)
    r = run_bass_kernel_spmd(nc, [arrays], core_ids=[0])
    return r.results[0]["y"]
```

```python
from contextlib import ExitStack

import concourse.bass as bass
from concourse import mybir

P = 128
F32 = mybir.dt.float32
F32R = mybir.dt.float32r
U32 = mybir.dt.uint32
ALU = mybir.AluOpType
ACT = mybir.ActivationFunctionType
AX = mybir.AxisListType

D = 2048
T = 512
TT = T // P
KD = D // P
CH = 1024
NH = 8
W = 31
NK = 128
TOPK = 16
PH = 8
ALPHA = 2.0 ** 0.25
LAM0 = 0.2
EPS = 1e-5

U1 = 8 * NH
U1T = 8
U2 = KD
U3 = KD
U4 = 2 * PH
U5 = 128
U6 = 128
U7 = 2
U8 = KD
B1 = 0
B1T = B1 + 2 * U1
B2 = B1T + 2 * U1T
B3 = B2 + 2 * U2
B4 = B3 + 2 * U3
B5 = B4 + 2 * U4
B6 = B5 + 2 * U5
B7 = B6 + 2 * U6
B8 = B7 + 2 * U7
NB = B8 + 2 * U8
NU = NB // 2
AHEAD = 4
FIRST_GATE_TAIL = 3 * NH

TD = T - P
NP = PH * TOPK
RT = 64
NRT = TD // RT
GT = RT // 4
PRE = 10
POST = PRE + 8 * NRT
RING = 4
TILE_GATHERS = [j % 4 != 3 for j in range(16)] + [j % 2 == 0 for j in range(16)]
POST_GATHERS = [j % 2 == 0 and j < 16 for j in range(4 * (64 - POST))]
GROUP_GATHERS = [j % 2 == 1 for j in range(16)]
GROUP0_GATHERS = [j >= 4 and j % 3 != 0 for j in range(16)]
NTG = sum(TILE_GATHERS)
assert NTG * NRT + sum(POST_GATHERS) == NP and NTG % RING == 0 and sum(GROUP_GATHERS) * 16 == NP

C_BIAS, C_LNG, C_LNB, C_SLOPE, NCPAR = W, W + 1, W + 2, W + 3, W + 5
V_LN1G, V_LN1B, V_LN2G, V_LN2B, V_PLEB, V_BG, V_SUB = 0, 16, 32, 48, 64, 80, 112
NPV = 113


def build(nc, ws, xT, pT, cpar, pvec, lamT, keysT, u_tab, v_tab, out):
    out2 = out.rearrange("b t d -> (b t) d")
    gate_sp = nc.dram_tensor("gate_spill", (2 * KD, P, T), F32).ap()
    x1_sp = nc.dram_tensor("x1_spill", (P, KD, T), F32).ap()
    gelu_sp = nc.dram_tensor("gelu_spill", (NK, P, TD), F32).ap()
    route_sp = nc.dram_tensor("route_spill", (NRT, P, NK * RT), F32).ap()

    with ExitStack() as ctx:
        def sem(name):
            return ctx.enter_context(nc.semaphore(name))

        KB = 1024
        base = 16512
        size = 212832 - 64
        ctx.enter_context(nc.sbuf_tensor("arena", [P, size // 4], F32))

        def at(name, offset, shape, dt=F32):
            n = 4
            for s in shape[1:]:
                n *= s
            assert offset + n <= size, (name, offset + n, size)
            return nc.alloc_sbuf_tensor_at(name, shape, dt, offset=base + offset)

        o_raw, o_whi, o_wlo, o_ahi, o_alo, o_r, o_s, o_c = [
            k * KB for k in (0, 16, 32, 48, 80, 112, 144, 176)]
        raw = at("raw", o_raw, [P, 2, 2, 1024])
        whi = at("whi", o_whi, [P, 4, 1024], F32R)
        wlo = at("wlo", o_wlo, [P, 4, 1024], F32R)
        ahi = at("ahi", o_ahi, [P, KD, T], F32R)
        alo = at("alo", o_alo, [P, KD, T], F32R)
        xin = at("xin", o_r, [P, KD, T])
        oThi = at("oThi", o_r, [P, NH, T], F32R)
        oTlo = at("oTlo", o_r + 16 * KB, [P, NH, T], F32R)
        res = at("res", o_r, [P, KD, T])
        gst = at("gst", o_r, [P, NK * RT])
        x1n = at("x1n", o_alo, [P, KD, T])
        urows = at("urows", o_s, [P, RING, D])
        vrows = at("vrows", o_alo, [P, RING, D])
        swhi = at("swhi", o_s, [P, NH, T], F32R)
        conv = at("conv", o_s + 16 * KB, [P, NH, T])
        swlo = at("swlo", o_s + 16 * KB, [P, NH, T], F32R)
        xwhi = [at(f"xwhi{i}", o, [P, 8, TD], F32R) for i, o in enumerate((o_s, o_ahi))]
        xwlo = [at(f"xwlo{i}", o + 12 * KB, [P, 8, TD], F32R) for i, o in enumerate((o_s, o_ahi))]
        yacc = at("yacc", o_s + 24 * KB, [P, D])
        phi = at("phi", o_ahi + 24 * KB, [P, 2, T], F32R)
        plo = at("plo", o_ahi + 28 * KB, [P, 2, T], F32R)
        eT = at("eT", o_s, [P, KD, T])

        c = [o_c]

        def small(name, shape, dt=F32):
            n = 4
            for s in shape[1:]:
                n *= s
            t = at(name, c[0], shape, dt)
            c[0] += (n + 31) // 32 * 32
            return t

        ident = small("ident", [P, P])
        ones = small("ones", [P, P])
        iota = small("iota", [P, NK])
        par = small("par", [P, NH, NCPAR])
        pv = small("pv", [P, NPV])
        lamv = small("lamv", [64, 4])
        lamp = small("lamp", [64, 2])
        lame = small("lame", [P, 2])
        nlam = small("nlam", [P, 1])
        sub8 = small("sub8", [P, 1])
        eps = small("eps", [P, 1])
        o_phase = c[0]

        glu = small("glu", [P, W - 1 + T])
        sg = small("sg", [P, T])
        sc = small("sc", [P, 2, T])
        aN = small("aN", [P, T])
        cur = small("cur", [P, NCPAR])
        nmx = small("nmx", [P, 2])
        sums = small("sums", [P, 2])
        rcp = small("rcp", [P, 2])
        rl = small("rl", [P, 1])
        ssq = small("ssq", [P, TT])
        rms = small("rms", [P, TT])
        rrms = small("rrms", [P, TT])
        assert c[0] <= o_phase + 12 * KB
        acc = sc[:, 0]
        o_after_ln = o_phase + 12 * KB
        c[0] = o_after_ln
        gout = small("gout", [P, 2, T])
        on = small("on", [P, T])
        oTf = small("oTf", [P, T])
        junk = small("junk", [P, P])
        c[0] = o_s
        qT = small("qT", [P, T])
        kT = small("kT", [P, T])
        vT = small("vT", [P, T])
        vn = small("vn", [P, TT, P])
        nd = small("nd", [P, T])
        aT = small("aT", [P, 2, T])
        assert c[0] <= o_s + 16 * KB

        c[0] = o_phase
        sq = small("sq", [P, 2, T])
        std = small("std", [P, T])
        rstd = small("rstd", [P, T])
        nrm = small("nrm", [P, 2, T])
        assert c[0] <= o_after_ln
        c[0] = o_after_ln
        gl = small("gl", [P, 2, 2, T])
        mt = small("mt", [P, T])
        xr = small("xr", [P, 2, T])
        msum = small("msum", [P, T])
        assert c[0] <= size
        keys = at("keys", o_after_ln, [P, 2 * PH, NK])
        c[0] = o_phase
        s4 = small("s4", [P, TT, NK])
        s4b = small("s4b", [P, TT, NK])
        cand = small("cand", [P, TT, TOPK * TOPK])
        assert c[0] <= o_after_ln
        c[0] = o_after_ln + 8 * KB
        qs = small("qs", [P, 2, T])
        assert c[0] <= size
        c[0] = o_s
        top = small("top", [P, 2, TT, TOPK])
        topi = small("topi", [P, 2, TT, TOPK], U32)
        best = small("best", [P, TT, PH, TOPK])
        bpos = small("bpos", [P, TT, PH, TOPK], U32)
        k1f = small("k1f", [P, TT, PH, TOPK])
        k2f = small("k2f", [P, TT, PH, TOPK])
        cand2 = small("cand2", [P, TT, TOPK * TOPK])
        bnow = small("bnow", [P, TT, TOPK])
        pnow = small("pnow", [P, TT, TOPK], U32)
        pab = small("pab", [P, 2, TT, TOPK], U32)
        pabf = small("pabf", [P, 2, TT, TOPK])
        know = small("know", [P, 2, TT, TOPK])
        hot = small("hot", [P, TT, TOPK, TOPK])
        pick = small("pick", [P, TT, TOPK])
        i1n = small("i1n", [P, TT, PH, TOPK])
        i2n = small("i2n", [P, TT, PH, TOPK])
        gn = small("gn", [P, TT, PH, TOPK])
        gsum = small("gsum", [P, TT * PH])
        grcp = small("grcp", [P, TT * PH])
        assert c[0] <= o_c
        c[0] = o_phase
        gd = small("gd", [P, NP])
        idf = small("idf", [P, NP])
        idx = small("idx", [P, NP], U32)
        hd = small("hd", [P, NP])
        idxs = small("idxs", [P, RING, 8], U32)
        o_route = c[0]
        i1T = small("i1T", [P, TD])
        i2T = small("i2T", [P, TD])
        ghi = small("ghi", [P, TD], F32R)
        glo = small("glo", [P, TD], F32R)
        hot1 = small("hot1", [P, 2, 4, P], F32R)
        hot2w = small("hot2w", [P, 2, 4, 2, P], F32R)
        o_route_end = c[0]
        c[0] = max(c[0], o_after_ln + 8 * KB)
        hst = small("hst", [P, 2, TD])
        msum2 = at("msum2", c[0] - 3 * KB, [P, T])
        o_p = c[0]
        assert c[0] <= size
        c[0] = o_route
        hg = small("hg", [P, 2, 2, 2 * TD])
        wt = small("wt", [P, TD])
        assert c[0] <= o_route_end
        c[0] = o_p
        hot2 = at("hot2", c[0], [P, 2, 4, P])
        pin = small("pin", [P, 2, T])
        assert c[0] <= size
        c[0] = o_after_ln
        sig = small("sig", [P, 2, T])
        yT = small("yT", [P, 2, T])
        yn = small("yn", [P, 2, TT, P])
        assert c[0] <= size

        ps = [ctx.enter_context(nc.psum_tensor(f"bank{i}", [P, T], F32)) for i in range(8)]
        ps_t, ps_s, ps_x, ps_o = ps[2:4], ps[4:6], ps[6], ps[7]
        ps_g = (ps[2:4], ps[4:6])

        raw_in = [sem("raw_in0"), sem("raw_in1")]
        hi_done = sem("hi_done")
        lo_done = sem("lo_done")
        blk_done = sem("blk_done")
        par_in = sem("par_in")
        x_in = [sem(f"x_in{i}") for i in range(KD // 2)]
        const_ok = sem("const_ok")
        x_hi = sem("x_hi")
        x_pair = sem("x_pair")
        lam_prod = sem("lam_prod")
        lam_sum = sem("lam_sum")
        lam_exp = sem("lam_exp")
        setup_ok = sem("setup_ok")
        evac1 = sem("evac1")
        s_full = sem("s_full")
        s_free = sem("s_free")
        max_ok = sem("max_ok")
        exp_ok = sem("exp_ok")
        a_ok = sem("a_ok")
        vtr_full = sem("vtr_full")
        vn_ok = sem("vn_ok")
        t_full = sem("t_full")
        aT_ok = sem("aT_ok")
        o_full = sem("o_full")
        rms_ok = sem("rms_ok")
        on_ok = sem("on_ok")
        oT_full = sem("oT_full")
        oT_hi = sem("oT_hi")
        oT_lo = sem("oT_lo")
        sg_ok = sem("sg_ok")
        gate_out = [sem(f"gate_out{i}") for i in range(2)]
        ln = [{n: sem(f"{n}{i}") for n in ("mean", "cent", "sqr", "sqr_used", "std_ok", "scaled", "affine", "hi_ok", "lo_ok", "sum")} for i in range(3)]
        evac2 = sem("evac2")
        gl_in = [sem("gl_in0"), sem("gl_in1")]
        mix_ok = sem("mix_ok")
        xr_in = [sem("xr_in0"), sem("xr_in1")]
        res_ok = sem("res_ok")
        keys_in = sem("keys_in")
        evac4 = sem("evac4")
        sc_full = sem("sc_full")
        sc_free = sem("sc_free")
        x1_out = sem("x1_out")
        soft_in = sem("soft_in")
        soft_exp = sem("soft_exp")
        picks_ok = sem("picks_ok")
        picks_full = sem("picks_full")
        evac5 = sem("evac5")
        hot_ok = sem("hot_ok")
        hot_scaled = sem("hot_scaled")
        g_full = sem("g_full")
        g_evac = sem("g_evac")
        gelu_out = [sem("gelu_out0"), sem("gelu_out1")]
        tile_out = sem("tile_out")
        x1_in = sem("x1_in")
        hg_in = [sem(f"hg_in{i}") for i in range(2)]
        x1t_full = sem("x1t_full")
        x1n_ok = sem("x1n_ok")
        idx_ok = sem("idx_ok")
        rows_in = [sem(f"rows_in{i}") for i in range(RING)]
        dots_ok = sem("dots_ok")
        hd_gelu = sem("hd_gelu")
        yacc_ok = sem("yacc_ok")
        yacc_full = sem("yacc_full")
        yacc_used = sem("yacc_used")
        w_ok = sem("w_ok")
        evac6 = sem("evac6")
        p_in = sem("p_in")
        p_ok = sem("p_ok")
        evac7 = sem("evac7")
        evac8 = sem("evac8")
        y_ok = sem("y_ok")
        yT_full = sem("yT_full")
        yn_ok = sem("yn_ok")
        out_done = [sem("out_done0"), sem("out_done1")]

        block = ctx.enter_context(nc.Block())

        @block.sync
        def _(sp):
            def load_unit(u, s):
                nxt = sp.snap(u + 2)
                sp.wait_ge(lo_done, 2 * u + 2)
                sp.dma_start(raw[:, s], ws[nxt]).then_inc(raw_in[s], 16)

            sp.dma_start(par[:], cpar).then_inc(par_in, 16)
            sp.dma_start(pv[:], pvec).then_inc(par_in, 16)
            sp.dma_start(lamv[:], lamT).then_inc(par_in, 16)
            sp.dma_start(raw[:, 0], ws[0]).then_inc(raw_in[0], 16)
            for q in range(KD // 2):
                sp.dma_start(xin[:, 2 * q:2 * q + 2], xT[:, 2 * q:2 * q + 2]).then_inc(x_in[q], 16)
            sp.dma_start(raw[:, 1], ws[1]).then_inc(raw_in[1], 16)

            with sp.Fori(0, (U1 + U1T) // 2) as i:
                for s in range(2):
                    load_unit(2 * i + s, s)

            def load_gates(j, s):
                j = sp.snap(j)
                sp.dma_start(gl[:, s, 0], gate_sp[j]).then_inc(gl_in[s], 16)
                sp.dma_start(gl[:, s, 1], gate_sp[j + KD]).then_inc(gl_in[s], 16)

            sp.wait_ge(ln[0]["lo_ok"], NH)
            sp.wait_ge(gate_out[0], 16 * (2 * NH + U1T // 2))
            sp.wait_ge(gate_out[1], 16 * (NH + U1T // 2))
            for s in range(2):
                load_gates(s, s)
            with sp.Fori(0, U2 // 2 - 1) as i:
                for s in range(2):
                    load_unit(2 * i + (B2 // 2 + s), s)
                    nxt = sp.snap(2 * i + s + 2)
                    sp.wait_ge(mix_ok, 2 * i + s + 1)
                    load_gates(nxt, s)
            for s in range(2):
                load_unit(B2 // 2 + U2 - 2 + s, s)

            def load_x(j, s):
                j = sp.snap(j)
                sp.dma_start(xr[:, s], xT[:, j]).then_inc(xr_in[s], 16)

            for s in range(2):
                load_x(s, s)
            sp.wait_ge(mix_ok, U2)
            sp.dma_start(keys[:], keysT).then_inc(keys_in, 16)
            with sp.Fori(0, U3 // 2 - 1) as i:
                for s in range(2):
                    load_unit(2 * i + (B3 // 2 + s), s)
                    nxt = sp.snap(2 * i + s + 2)
                    sp.wait_ge(res_ok, 2 * i + s + 1)
                    load_x(nxt, s)
            for s in range(2):
                load_unit(B3 // 2 + U3 - 2 + s, s)

            def spill_x1(q):
                sp.wait_ge(ln[1]["lo_ok"], 4 * q + 4)
                sp.dma_start(x1_sp[:, 4 * q:4 * q + 4], res[:, 4 * q:4 * q + 4]).then_inc(x1_out, 16)

            for s in range(2):
                load_unit(B4 // 2 + s, s)
            for q in range(4):
                spill_x1(q)
            with sp.Fori(1, U4 // 2) as i:
                for s in range(2):
                    load_unit(2 * i + (B4 // 2 + s), s)

            def expert_loads(first, n):
                with sp.Fori(0, n) as i:
                    for s in range(2):
                        load_unit(2 * i + first + (B5 // 2 + s), s)

            def tile_loads(t):
                expert_loads(2 * PRE + 16 * t, 5)
                tt = sp.snap(t)
                sp.wait_ge(g_evac, t * GT + (2 + GT))
                for q in range(6):
                    n = NK * RT // 4
                    if q < 4:
                        sp.dma_start(route_sp[tt, :, q * n:(q + 1) * n], gst[:, q * n:(q + 1) * n]
                                     ).then_inc(tile_out, 16)
                    load_unit(16 * t + (B5 // 2 + 2 * PRE + 10 + q), q % 2)

            def load_hg(k, s):
                k2 = sp.snap(k * 2)
                sp.dma_start(hg[:, s, 0].rearrange("p (c t) -> p c t", c=2),
                             gelu_sp[bass.ds(k2, 2)].rearrange("c p t -> p c t")).then_inc(hg_in[s], 16)
                kk = sp.snap(k * 2 * RT)
                sp.dma_start(hg[:, s, 1].rearrange("p (a x) -> p a x", a=NRT),
                             route_sp[:, :, bass.ds(kk, 2 * RT)].rearrange("a p x -> p a x")
                             ).then_inc(hg_in[s], 16)

            expert_loads(0, PRE)
            with sp.Fori(0, NRT) as t:
                tile_loads(t)
            for k in range(2 * (64 - POST)):
                load_unit(B5 // 2 + 2 * POST + k, k % 2)
                if k == 1:
                    sp.wait_ge(tile_out, 64 * NRT)
                    sp.wait_ge(g_full, TD // 4)
                    for s in range(2):
                        sp.wait_ge(gelu_out[s], 16 * 4)
                    sp.dma_start(pin[:], pT).then_inc(p_in, 16)
                if k in (2, 4):
                    load_hg(k // 2 - 1, k // 2 - 1)
                if k in (3, 5, 7, 11):
                    q = (3, 5, 7, 11).index(k)
                    sp.dma_start(res[:, 4 * q:4 * q + 4], x1_sp[:, 4 * q:4 * q + 4]).then_inc(x1_in, 16)
                if k in (9, 10):
                    sp.wait_ge(w_ok, 2 * (k - 7) - 2)
                    load_hg(k - 7, k - 9)

            def group_loads(g, first=False):
                for k in range(8):
                    load_unit(g * 8 + (B6 // 2 + k), k % 2)
                    if first and k in (0, 4):
                        for s in range(2):
                            sp.wait_ge(gelu_out[s], 16 * (6 if k == 0 else U5 // 2))
                    if k % 2 == 0:
                        kp = sp.snap(g * 4 + (4 + k // 2))
                        sp.wait_ge(w_ok, g * 8 + (8 + k - 2))
                        load_hg(kp, k // 2 % 2)

            group_loads(0, first=True)
            with sp.Fori(1, 15) as g:
                group_loads(g)
            for k in range(8):
                load_unit(B6 // 2 + 15 * 8 + k, k % 2)

            with sp.Fori(0, (U7 + U8) // 2 - 1) as i:
                for s in range(2):
                    load_unit(2 * i + (B7 // 2 + s), s)
            for s in range(2):
                sp.wait_ge(out_done[s], 16 * KD // 2)

        @block.gpsimd
        def _(pool):
            nc.gpsimd.memset(ones[:], 1.0)
            nc.gpsimd.memset(eps[:], EPS)
            nc.gpsimd.memset(ident[:], 0.0)
            nc.gpsimd.memset(glu[:, 0:W - 1], 0.0)
            nc.gpsimd.iota(iota[:], [[1, NK]], base=0, channel_multiplier=0,
                           allow_small_or_imprecise_dtypes=True)
            nc.gpsimd.iota(nd[:], [[1, T]], base=-(T - P), channel_multiplier=-1,
                           allow_small_or_imprecise_dtypes=True)
            pool.drain()
            nc.gpsimd.affine_select(out=ident[:], in_=ident[:], compare_op=ALU.not_equal, fill=1.0,
                                    base=0, pattern=[[-1, P]], channel_multiplier=1)
            nc.gpsimd.affine_select(out=nd[:], in_=nd[:], compare_op=ALU.is_ge, fill=-1e30,
                                    base=T - P, pattern=[[-1, T]], channel_multiplier=1)
            pool.drain().then_inc(const_ok, 1)

            def lo_part(b, s):
                pool.wait_ge(hi_done, b + 1)
                nc.gpsimd.tensor_tensor(wlo[:, s], raw[:, s // 2, s % 2], whi[:, s].bitcast(F32),
                                        ALU.subtract).then_inc(lo_done, 1)

            def lo_parts(first, n):
                with pool.Fori(0, n // 4) as i:
                    for s in range(4):
                        lo_part(4 * i + (first + s), s)

            def with_gathers(b, n, which, table, rows):
                for j, gather in enumerate(which):
                    if gather:
                        pool.wait_ge(idx_ok, n + 1)
                    lo_part(b + j, j % 4)
                    if gather:
                        s = sum(which[:j]) % RING
                        nc.gpsimd.indirect_dma_start(
                            rows[:, s], None, table,
                            bass.IndirectOffsetOnAxis(ap=idxs[:, s, 0:1], axis=0)).then_inc(rows_in[s], 16)
                        n = n + 1

            lo_parts(0, B5 + 4 * PRE)
            with pool.Fori(0, NRT) as t:
                with_gathers(32 * t + (B5 + 4 * PRE), NTG * t, TILE_GATHERS, u_tab, urows)
            with_gathers(B5 + 4 * POST, NTG * NRT, POST_GATHERS, u_tab, urows)
            with_gathers(B6, NP, GROUP0_GATHERS, v_tab, vrows)
            with pool.Fori(1, 16) as g:
                with_gathers(16 * g + B6, 8 * g + NP, GROUP_GATHERS, v_tab, vrows)
            lo_parts(B7, NB - B7)

        @block.tensor
        def _(pe):
            def three(ps_out, hi, lo, xh, xl, first, last):
                pe.matmul(ps_out, hi, xh, start=first, stop=False)
                pe.matmul(ps_out, hi, xl, start=False, stop=False)
                return pe.matmul(ps_out, lo, xh, start=False, stop=last)

            def one_block(b, s, bank, half, wait_x=None, n=T):
                pe.wait_ge(lo_done, b + 1)
                for k in range(8):
                    kk = 8 * half + k
                    if wait_x is not None:
                        pe.wait_ge(wait_x, kk + 1)
                    t = slice(k * P, (k + 1) * P)
                    mm = three(ps[bank][:, 0:n], whi[:, s, t], wlo[:, s, t], ahi[:, kk, 0:n],
                               alo[:, kk, 0:n], kk == 0, kk == KD - 1)
                mm.then_inc(blk_done, 1)

            def norm_mean(i, total):
                pe.wait_ge(ln[i]["sum"], 1)
                pe.matmul(ps_x[:], ones[:], total[:], start=True, stop=True).then_inc(ln[i]["mean"], 1)

            def first_units(b, wait_x):
                for half in range(2):
                    pe.wait_ge(lo_done, b + half + 3)
                    for k in range(8):
                        pe.wait_ge(wait_x, 8 * half + k + 1)
                        t, kk = slice(k * P, (k + 1) * P), 8 * half + k
                        for u in range(2):
                            mm = three(ps[u][:], whi[:, 2 * u + half, t], wlo[:, 2 * u + half, t],
                                       ahi[:, kk], alo[:, kk], kk == 0, kk == KD - 1)
                            if k == 7 and u == 0:
                                mm.then_inc(blk_done, 1)
                mm.then_inc(blk_done, 2)

            def norm_var(i, n):
                for k in range(n):
                    pe.wait_ge(ln[i]["sqr"], k + 1)
                    mm = pe.matmul(ps_o[:], ones[:], sq[:, k % 2], start=(k == 0), stop=(k == n - 1))
                    mm.then_inc(ln[i]["sqr_used"], 1)

            pe.wait_ge(const_ok, 1)
            pe.wait_ge(lam_prod, 1)
            pe.matmul(ps_x[:, 0:2], ones[0:64, :], lamp[:], start=True, stop=True).then_inc(lam_sum, 1)

            def scores(h, b):
                if b == 0:
                    pe.wait_ge(evac1, 8 * h + 4)
                else:
                    pe.wait_ge(s_free, 4 * h + b)
                for m in range(2):
                    r = slice(64 * m, 64 * m + 64)
                    mm = pe.matmul(ps_s[m][:, 0:(b + 1) * P], qT[r, b * P:(b + 1) * P],
                                   kT[r, 0:(b + 1) * P], start=True, stop=True)
                mm.then_inc(s_full, 1)

            def turn_v(h):
                pe.wait_ge(evac1, 8 * h + 5)
                for k in range(TT):
                    mm = pe.transpose(ps_o[:, k * P:(k + 1) * P], vT[:, k * P:(k + 1) * P], ident[:])
                mm.then_inc(vtr_full, 1)

            def turn_a(h, b):
                pe.wait_ge(a_ok, 4 * h + b + 1)
                if b >= 2:
                    pe.wait_ge(aT_ok, 4 * h + b - 1)
                for k in range(b + 1):
                    mm = pe.transpose(ps_t[b % 2][:, k * P:(k + 1) * P], aN[:, k * P:(k + 1) * P], ident[:])
                mm.then_inc(t_full, 1)

            def weigh_v(h, b):
                if b == 0:
                    pe.wait_ge(vn_ok, h + 1)
                pe.wait_ge(aT_ok, 4 * h + b + 1)
                for k in range(b + 1):
                    mm = pe.matmul(ps_o[:, b * P:(b + 1) * P], aT[:, b % 2, k * P:(k + 1) * P],
                                   vn[:, k], start=(k == 0), stop=(k == b))
                if b == TT - 1:
                    mm.then_inc(o_full, 1)

            def turn_o(h):
                pe.wait_ge(on_ok, h + 1)
                for k in range(TT):
                    mm = pe.transpose(ps_x[:, k * P:(k + 1) * P], on[:, k * P:(k + 1) * P], ident[:])
                mm.then_inc(oT_full, 1)

            pe.wait_ge(setup_ok, 1)
            def head(h, first=False):
                for n in range(16):
                    if n % 2 == 0:
                        pe.wait_ge(evac1, 8 * h + n // 2 + 1)
                    one_block(16 * h + n, n % 4, n // 2 % 2, n % 2,
                              wait_x=x_pair if first and n < 2 else None)
                    if n == 2 and not first:
                        turn_o(h - 1)
                    if n == 4:
                        scores(h, 0)
                    if n == 6:
                        turn_v(h)
                        scores(h, 1)
                    if n == 7:
                        turn_a(h, 0)
                    if n == 8:
                        scores(h, 2)
                    if n == 9:
                        weigh_v(h, 0)
                        turn_a(h, 1)
                    if n == 10:
                        scores(h, 3)
                    if n == 11:
                        weigh_v(h, 1)
                        turn_a(h, 2)
                    if n == 12:
                        turn_a(h, 3)
                    if n == 13:
                        weigh_v(h, 2)
                        weigh_v(h, 3)

            head(0, first=True)
            with pe.Fori(1, NH) as h:
                head(h)
            for n in range(2 * U1T):
                if n % 2 == 0:
                    pe.wait_ge(evac1, U1 + n // 2 + 1)
                one_block(B1T + n, n % 4, n // 2 % 2, n % 2)
                if n == 1:
                    turn_o(NH - 1)
                if n == 3:
                    pe.wait_ge(oT_hi, NH)
                    norm_mean(0, msum)
                if n == 5:
                    norm_var(0, NH)

            def branch_unit(j, s, wait_x=False):
                for half, (xh, xl) in enumerate(((swhi, swlo), (oThi, oTlo))):
                    pe.wait_ge(lo_done, 2 * j + (B2 + half + 1))
                    for k in range(8):
                        if wait_x and half == 0:
                            pe.wait_ge(ln[0]["lo_ok"], k + 1)
                        t = slice(k * P, (k + 1) * P)
                        w = 2 * s + half
                        mm = three(ps[w][:], whi[:, w, t], wlo[:, w, t], xh[:, k], xl[:, k], k == 0, k == 7)
                    mm.then_inc(blk_done, 1)

            pe.wait_ge(evac1, 2 + U1 + U1T)
            pe.wait_ge(oT_lo, NH)
            for s in range(2):
                branch_unit(s, s, wait_x=(s == 0))
            with pe.Fori(1, U2 // 2) as i:
                for s in range(2):
                    pe.wait_ge(evac2, 2 * i + s - 1)
                    branch_unit(2 * i + s, s)

            def out_unit(j, s, first=False):
                if not first:
                    pe.wait_ge(res_ok, j - 1)
                for half in range(2):
                    one_block(2 * j + (B3 + half), 2 * s + half, s, half,
                              wait_x=mix_ok if first and s == 0 else None)

            pe.wait_ge(evac2, U2)
            out_unit(0, 0, first=True)
            out_unit(1, 1, first=True)
            with pe.Fori(1, U3 // 2) as i:
                for s in range(2):
                    out_unit(2 * i + s, s)
            norm_mean(1, msum)
            norm_var(1, KD)

            def key_scores(hc, s):
                pe.wait_ge(evac4, hc + 1)
                for a in range(TT):
                    mm = pe.matmul(ps_s[s][:, a * P:(a + 1) * P], qs[:, s, a * P:(a + 1) * P],
                                   keys[:, hc], start=True, stop=True)
                mm.then_inc(sc_full, 1)

            def query_pair(i, second=False):
                for s in range(2):
                    for half in range(2):
                        one_block(4 * i + (B4 + 2 * s + half), 2 * s + half, s, half)
                        if second and s == 0 and half == 0:
                            pe.wait_ge(sc_free, 1)
                            key_scores(0, 0)
                        if half == 0:
                            pe.wait_ge(sc_free, 2 * i + s)
                            key_scores(2 * i + (s - 1), 1 - s)

            pe.wait_ge(res_ok, KD)
            pe.wait_ge(keys_in, 16)
            first_units(B4, ln[1]["lo_ok"])
            pe.wait_ge(evac4, 1)
            query_pair(1, second=True)
            with pe.Fori(2, PH) as i:
                query_pair(i)

            def turn_picks():
                pe.wait_ge(picks_ok, 1)
                for dst, src in ((ps_s[0], gn), (ps_s[1], i1n), (ps_x, i2n)):
                    for a in range(TD // P):
                        mm = pe.transpose(dst[:, a * P:(a + 1) * P],
                                          src[:, a].rearrange("p h k -> p (h k)"), ident[:])
                mm.then_inc(picks_full, 1)

            def route(g, s):
                pe.wait_ge(hot_scaled, g + 1)
                pe.wait_ge(g_evac, g + 1)
                for k in range(4):
                    mm = pe.matmul(ps_g[s][k // 2][:, k % 2 * 2 * P:(k % 2 + 1) * 2 * P], hot1[:, s, k],
                                   hot2w[:, s, k].rearrange("p c k -> p (c k)"), start=True, stop=True)
                mm.then_inc(g_full, 1)

            def expert_step(i, g=None):
                for s in range(2):
                    pe.wait_ge(evac5, i * 2 + (s + 1))
                    for half in range(2):
                        one_block(i * 4 + (B5 + 2 * s + half), 2 * s + half, s, half, n=TD)
                        if g is not None:
                            route(g + (2 * s + half), half)

            pe.wait_ge(evac4, U4)
            pe.wait_ge(sc_free, U4)
            key_scores(U4 - 1, 1)
            for q in range(4):
                for k in range(4):
                    mm = pe.transpose(ps[(2, 3, 6, 7)[q]][:, k * P:(k + 1) * P],
                                      res[:, 4 * q + k, TD:T], ident[:])
            mm.then_inc(x1t_full, 1)
            with pe.Fori(0, PRE) as i:
                expert_step(i)
            pe.wait_ge(sc_free, U4 + 2)
            pe.wait_ge(x1n_ok, 4)
            turn_picks()
            with pe.Fori(0, NRT) as t:
                t = pe.snap(t)
                with pe.Fori(0, 4) as i:
                    expert_step(8 * t + i + PRE, GT * t + 4 * i)
                with pe.Fori(4, 8) as i:
                    expert_step(8 * t + i + PRE)
            with pe.Fori(POST, 64) as i:
                expert_step(i)

            def value_group(g, q):
                pe.wait_ge(w_ok, g * 8 + 8)
                for u in range(8):
                    pe.wait_ge(evac6, g * 8 + (u + 1))
                    for half in range(2):
                        b, s = g * 16 + (B6 + 2 * u + half), 2 * (u % 2) + half
                        pe.wait_ge(lo_done, b + 1)
                        for k in range(8):
                            t = slice(k * P, (k + 1) * P)
                            mm = three(ps[s][:, 0:TD], whi[:, s, t], wlo[:, s, t],
                                       xwhi[q][:, k], xwlo[q][:, k], k == 0, k == 7)
                        mm.then_inc(blk_done, 1)

            pe.wait_ge(evac5, 2 + U5)
            pe.wait_ge(g_evac, 2 + TD // 4)
            with pe.Fori(0, 8) as i:
                for q in range(2):
                    value_group(2 * i + q, q)

            def project(n, first_bank, after=None):
                pe.wait_ge(lo_done, B7 + n + 1)
                for j in range(4):
                    if n == 1:
                        pe.wait_ge(yacc_used, j + 1)
                    for k in range(2):
                        t = slice((2 * j + k) * P, (2 * j + k + 1) * P)
                        mm = three(ps[first_bank + j][:], whi[:, n, t], wlo[:, n, t],
                                   phi[:, k], plo[:, k], k == 0, k == 1)
                    if j == 1 and after is not None:
                        after()
                mm.then_inc(blk_done, 1)

            def mean_of_x2():
                pe.wait_ge(evac7, 8)
                norm_mean(2, msum2)

            pe.wait_ge(evac6, 2 + U6)
            pe.wait_ge(p_ok, 1)
            project(0, 0)
            pe.wait_ge(yacc_ok, 1)
            for q in range(4):
                for k in range(4):
                    d = slice((4 * q + k) * P, (4 * q + k + 1) * P)
                    mm = pe.transpose(ps[4 + q][:, k * P:(k + 1) * P], yacc[:, d], ident[:])
            mm.then_inc(yacc_full, 1)
            project(1, 4)
            pe.wait_ge(evac7, 4)
            project(2, 0, after=mean_of_x2)
            norm_var(2, KD)
            pe.wait_ge(evac7, 12)
            project(3, 2)

            def turn_y(m, s):
                pe.wait_ge(y_ok, m + 1)
                pe.wait_ge(yn_ok, m + 1)
                for a in range(TT):
                    mm = pe.transpose(ps_t[s][:, a * P:(a + 1) * P], yT[:, s, a * P:(a + 1) * P], ident[:])
                mm.then_inc(yT_full, 1)

            def ple_pair(i, second=False):
                for s in range(2):
                    pe.wait_ge(evac8, 2 * i + (s - 1))
                    for half in range(2):
                        one_block(4 * i + (B8 + 2 * s + half), 2 * s + half, s, half)
                        if second and s == 0:
                            turn_y(half, half)
                        elif half == 0:
                            turn_y(2 * i + (s - 1), 1 - s)

            first_units(B8, ln[2]["lo_ok"])
            pe.wait_ge(evac7, KD)
            ple_pair(1, second=True)
            with pe.Fori(2, U8 // 2) as i:
                ple_pair(i)
            turn_y(U8 - 1, 1)

        @block.scalar
        def _(act):
            def hi_part(b, s, unit=None):
                nxt = b + AHEAD
                act.wait_ge(blk_done, b + 1)
                act.wait_ge(raw_in[s // 2], unit)
                act.activation(whi[:, s], raw[:, s // 2, s % 2], ACT.Copy).then_inc(hi_done, 1)

            def step(b, s):
                hi_part(b, s, (b - s) * 4 + 32)

            def norm_squares(i, n, src):
                for k in range(n):
                    act.wait_ge(ln[i]["cent"], k + 1)
                    if k >= 2:
                        act.wait_ge(ln[i]["sqr_used"], k - 1)
                    act.activation(sq[:, k % 2], src[:, k], ACT.Square).then_inc(ln[i]["sqr"], 1)
                act.wait_ge(ln[i]["sqr_used"], n)
                act.activation(std[:], ps_o[:], ACT.Sqrt, bias=eps[:], scale=1.0 / (n * P)
                               ).then_inc(ln[i]["std_ok"], 1)

            def norm_affine(i, n, dst, hi, func, gain, bias, between=None):
                for k in range(n):
                    if between is not None:
                        between(k)
                    act.wait_ge(ln[i]["scaled"], k + 1)
                    act.activation(dst[:, k], nrm[:, k % 2], func, bias=bias(k), scale=gain(k)
                                   ).then_inc(ln[i]["affine"], 1)
                    act.drain()
                    act.activation(hi[:, k], dst[:, k], ACT.Copy).then_inc(ln[i]["hi_ok"], 1)

            act.sem_inc(evac1, 2)
            act.sem_inc(evac5, 2)
            act.sem_inc(yn_ok, 2)
            act.wait_ge(lam_sum, 1)
            act.activation(lame[:], ps_x[:, 0:2], ACT.Exp).then_inc(lam_exp, 1)
            for s in range(4):
                if s == 2:
                    for q in range(KD // 2):
                        act.wait_ge(x_in[q], 16)
                        act.activation(ahi[:, 2 * q:2 * q + 2], xin[:, 2 * q:2 * q + 2], ACT.Copy
                                       ).then_inc(x_hi, 1)
                act.wait_ge(raw_in[s // 2], 16)
                act.activation(whi[:, s], raw[:, s // 2, s % 2], ACT.Copy).then_inc(hi_done, 1)
            act.wait_ge(setup_ok, 1)

            def softmax_exp(h, b):
                act.wait_ge(max_ok, 4 * h + b + 1)
                n = (b + 1) * P
                for m in range(2):
                    e = act.activation(sc[:, m, 0:n], sc[:, m, 0:n], ACT.Exp, bias=nmx[:, m:m + 1],
                                       accum_out=sums[:, m:m + 1])
                act.drain().then_inc(exp_ok, 1)

            def take_aT(h, b):
                act.wait_ge(t_full, 4 * h + b + 1)
                n = (b + 1) * P
                act.copy(aT[:, b % 2, 0:n], ps_t[b % 2][:, 0:n]).then_inc(aT_ok, 1)

            def take_gate(g, bank, slot):
                act.activation(gout[:, slot], ps[bank][:], ACT.Sigmoid, bias=pv[:, bass.ds(g + V_BG, 1)]
                               ).then_inc(evac1, 1)
                act.drain()
                act.dma_start(gate_sp[g], gout[:, slot]).then_inc(gate_out[slot], 16)

            def take_o(h):
                act.wait_ge(oT_full, h + 1)
                act.activation(oTf[:], ps_x[:], ACT.Copy, scale=sub8[:])
                act.drain()
                act.activation(oThi[:, h], oTf[:], ACT.Copy).then_inc(oT_hi, 1)

            def head(h, first=False):
                for n in range(16):
                    step(16 * h + n, n % 4)
                    if n == 3 and not first:
                        take_o(h - 1)
                    if n == 1:
                        act.mul(qT[:], ps[0][:], 0.125).then_inc(evac1, 1)
                    if n == 3:
                        act.copy(kT[:], ps[1][:]).then_inc(evac1, 1)
                    if n == 5:
                        act.copy(vT[:], ps[0][:]).then_inc(evac1, 1)
                        softmax_exp(h, 0)
                    if n == 6:
                        act.wait_ge(vtr_full, h + 1)
                        act.copy(vn[:].rearrange("p a b -> p (a b)"), ps_o[:]).then_inc(vn_ok, 1)
                    if n == 7:
                        act.copy(glu[:, W - 1:], ps[1][:]).then_inc(evac1, 1)
                        softmax_exp(h, 1)
                    if n == 8:
                        take_aT(h, 0)
                    if n == 9:
                        act.activation(sg[:], ps[0][:], ACT.Sigmoid).then_inc(evac1, 1)
                        act.drain().then_inc(sg_ok, 1)
                        softmax_exp(h, 2)
                    if n == 10:
                        take_aT(h, 1)
                    if n == 11:
                        softmax_exp(h, 3)
                        take_gate(3 * h, 1, 0)
                    if n == 12:
                        take_aT(h, 2)
                        take_aT(h, 3)
                    if n == 13:
                        take_gate(3 * h + 1, 0, 1)
                    if n == 14:
                        act.wait_ge(o_full, h + 1)
                        for b in range(TT):
                            if b:
                                act.drain()
                            act.activation(junk[:], ps_o[:, b * P:(b + 1) * P],
                                           ACT.Square, accum_out=ssq[:, b:b + 1])
                        act.drain()
                        act.activation(rms[:], ssq[:], ACT.Sqrt, bias=eps[:], scale=1.0 / P
                                       ).then_inc(rms_ok, 1)
                    if n == 15:
                        act.wait_ge(gate_out[0], 32 * h + 16)
                        take_gate(3 * h + 2, 1, 0)
                        act.wait_ge(gate_out[0], 32 * h + 32)
                        act.wait_ge(gate_out[1], 16 * h + 16)

            head(0, first=True)
            with act.Fori(1, NH) as h:
                head(h)
            for n in range(2 * U1T):
                step(B1T + n, n % 4)
                if n % 2 == 1:
                    u = n // 2
                    if u >= 2:
                        act.wait_ge(gate_out[u % 2], (2 - u % 2) * 16 * NH + 16 * (u // 2))
                    take_gate(FIRST_GATE_TAIL + u, u % 2, u % 2)
                if n == 2:
                    take_o(NH - 1)
                if n == 4:
                    norm_squares(0, NH, conv)
                if n == 8:
                    norm_affine(0, NH, conv, swhi, ACT.Silu,
                                lambda k: par[:, k, C_LNG:C_LNG + 1], lambda k: par[:, k, C_LNB:C_LNB + 1])

            with act.Fori(0, (U2 + U3) // 2) as i:
                for s in range(4):
                    step(4 * i + (B2 + s), s)
            norm_squares(1, KD, res)
            norm_affine(1, KD, res, ahi, ACT.Identity,
                        lambda k: pv[:, V_LN1G + k:V_LN1G + k + 1], lambda k: pv[:, V_LN1B + k:V_LN1B + k + 1])

            with act.Fori(0, PH) as i:
                for s in range(4):
                    step(4 * i + (B4 + s), s)
                    if s % 2 == 1:
                        act.copy(qs[:, s // 2], ps[s // 2][:]).then_inc(evac4, 1)

            def scale_hots(g, s):
                act.wait_ge(hot_ok, g + 1)
                for k in range(4):
                    tok = bass.ds(4 * g + k, 1)
                    act.activation(hot2w[:, s, k, 0], hot2[:, s, k], ACT.Copy, scale=ghi[:, tok].bitcast(F32))
                    sc2 = act.activation(hot2w[:, s, k, 1], hot2[:, s, k], ACT.Copy,
                                         scale=glo[:, tok].bitcast(F32))
                sc2.then_inc(hot_scaled, 1)

            def expert_step(i, first=False, group=None, groups=4):
                for s in range(4):
                    step(i * 4 + (B5 + s), s)
                    if s % 2 == 1:
                        u = s // 2
                        if not (first and u == 0):
                            act.wait_ge(gelu_out[1 - u], i * 16 + 16 * u)
                        act.activation(hst[:, u], ps[u][:, 0:TD], ACT.Gelu_apprx_tanh).then_inc(evac5, 1)
                        act.drain()
                        act.dma_start(gelu_sp[i * 2 + u], hst[:, u]).then_inc(gelu_out[u], 16)
                    if group is not None and s < groups:
                        scale_hots(group + s, s % 2)

            def routing_tile(t):
                for g in range(2):
                    scale_hots(GT * t + g, g)
                with act.Fori(0, 3) as i:
                    expert_step(8 * t + i + PRE, group=GT * t + 4 * i + 2)
                expert_step(8 * t + (PRE + 3), group=GT * t + 14, groups=2)
                with act.Fori(4, 8) as i:
                    expert_step(8 * t + i + PRE)

            act.wait_ge(x1t_full, 1)
            for q in range(4):
                act.copy(x1n[:, 4 * q:4 * q + 4, TD:T],
                         ps[(2, 3, 6, 7)[q]][:].rearrange("p (k d) -> p k d", k=4)).then_inc(x1n_ok, 1)
            expert_step(0, first=True)
            with act.Fori(1, PRE - 1) as i:
                expert_step(i)
            act.wait_ge(soft_in, 1)
            act.activation(gn[:], gn[:], ACT.Exp).then_inc(soft_exp, 1)
            expert_step(PRE - 1)
            with act.Fori(0, NRT) as t:
                routing_tile(act.snap(t))
            with act.Fori(POST, 64) as i:
                expert_step(i)
            act.wait_ge(dots_ok, 1)
            act.activation(hd[:], hd[:], ACT.Gelu_apprx_tanh).then_inc(hd_gelu, 1)

            with act.Fori(0, U6 // 2) as i:
                for s in range(4):
                    step(4 * i + (B6 + s), s)

            def take_e(n, first_bank):
                for j in range(4):
                    act.copy(eT[:, 4 * n + j], ps[first_bank + j][:]).then_inc(evac7, 1)

            for n in range(3):
                step(B7 + n, n)
                take_e(n, 4 * (n % 2))
            norm_squares(2, KD, res)
            norm_affine(2, KD, res, ahi, ACT.Identity,
                        lambda k: pv[:, V_LN2G + k:V_LN2G + k + 1], lambda k: pv[:, V_LN2B + k:V_LN2B + k + 1],
                        between=lambda k: step(B7 + 3, 3) if k == 4 else None)
            take_e(3, 2)

            def take_y(m, s, first=False):
                act.wait_ge(yT_full, m + 1)
                if not first:
                    act.wait_ge(out_done[1 - s], (m + s) * 8)
                act.copy(yn[:, s].rearrange("p a b -> p (a b)"), ps_t[s][:]).then_inc(yn_ok, 1)
                act.drain()
                act.dma_start(out2.rearrange("(a p) (j d) -> j p a d", p=P, d=P)[m], yn[:, s]
                              ).then_inc(out_done[s], 16)

            def ple_pair(i, first=False, last=False):
                for s in range(4):
                    b = 4 * i + (B8 + s)
                    if last:
                        act.wait_ge(blk_done, b + 1)
                    else:
                        step(b, s)
                    if s % 2 == 0 and not (first and s == 0):
                        m, ms = 2 * i + (s // 2 - 1), 1 - s // 2
                        take_y(m, ms, first and s == 2)
                    if s % 2 == 1:
                        u = s // 2
                        act.activation(sig[:, u], ps[u][:], ACT.Sigmoid,
                                       bias=pv[:, bass.ds(2 * i + (V_PLEB + u), 1)]).then_inc(evac8, 1)

            ple_pair(0, first=True)
            with act.Fori(1, U8 // 2 - 1) as i:
                ple_pair(i)
            ple_pair(U8 // 2 - 1, last=True)
            take_y(U8 - 1, 1)

        @block.vector
        def _(dve):
            dve.sem_inc(sc_free, 2)
            dve.sem_inc(evac6, 2)
            dve.sem_inc(g_evac, 2)
            dve.wait_ge(par_in, 48)
            dve.tensor_tensor(lamp[:], lamv[:, 0:4:2], lamv[:, 1:4:2], ALU.mult).then_inc(lam_prod, 1)
            dve.tensor_scalar(sub8[:], pv[:, V_SUB:V_SUB + 1], 1.0 - LAM0, None, ALU.mult)
            dve.wait_ge(lam_exp, 1)
            dve.tensor_tensor(nlam[:], lame[:, 1:2], lame[:, 0:1], ALU.subtract)
            dve.drain()
            dve.tensor_scalar(nlam[:], nlam[:], -LAM0, None, ALU.add)
            dve.wait_ge(const_ok, 1)
            dve.drain().then_inc(setup_ok, 1)
            for q in range(KD // 2):
                k = slice(2 * q, 2 * q + 2)
                dve.wait_ge(x_hi, q + 1)
                dve.tensor_tensor(alo[:, k], xin[:, k], ahi[:, k].bitcast(F32), ALU.subtract
                                  ).then_inc(x_pair, 2)

            def attention_weights(h, b):
                n = (b + 1) * P
                dve.drain()
                dve.wait_ge(s_full, 4 * h + b + 1)
                for m in range(2):
                    st = dve.scalar_tensor_tensor(sc[:, m, 0:n], nd[:, T - n:], cur[:, C_SLOPE:C_SLOPE + 1],
                                                  ps_s[m][:, 0:n], ALU.mult, ALU.add)
                st.then_inc(s_free, 1)
                dve.drain()
                dve.tensor_reduce(nmx[:], sc[:, :, 0:n], AX.X, ALU.max, negate=True).then_inc(max_ok, 1)
                dve.wait_ge(exp_ok, 4 * h + b + 1)
                dve.reciprocal(rcp[:], sums[:])
                dve.drain()
                dve.tensor_tensor(rl[:], rcp[:, 1:2], nlam[:], ALU.mult)
                dve.drain()
                dve.tensor_scalar(sc[:, 1, 0:n], sc[:, 1, 0:n], rl[:], None, ALU.mult)
                dve.drain()
                if b >= 1:
                    dve.wait_ge(t_full, 4 * h + b)
                dve.scalar_tensor_tensor(aN[:, 0:n], sc[:, 0, 0:n], rcp[:, 0:1], sc[:, 1, 0:n],
                                         ALU.mult, ALU.add).then_inc(a_ok, 1)

            def o_low(h):
                dve.wait_ge(oT_hi, h + 1)
                dve.tensor_tensor(oTlo[:, h], oTf[:], oThi[:, h].bitcast(F32), ALU.subtract
                                  ).then_inc(oT_lo, 1)

            def head(h, first=False):
                dve.drain()
                dve.tensor_copy(cur[:], par[:, h])
                dve.drain()
                for b in range(TT):
                    attention_weights(h, b)
                    if b == 0 and not first:
                        o_low(h - 1)
                dve.wait_ge(sg_ok, h + 1)
                dve.tensor_tensor(glu[:, W - 1:], glu[:, W - 1:], sg[:], ALU.mult)
                dve.drain()
                dve.tensor_scalar(acc, glu[:, 0:T], cur[:, 0:1], cur[:, C_BIAS:C_BIAS + 1],
                                  ALU.mult, ALU.add)
                for w in range(1, W):
                    dve.drain()
                    dst = acc if w < W - 1 else conv[:, h]
                    dve.scalar_tensor_tensor(dst, glu[:, w:w + T], cur[:, w:w + 1], acc,
                                             ALU.mult, ALU.add)
                dve.drain()
                if first:
                    dve.tensor_copy(msum[:], conv[:, h])
                else:
                    dve.tensor_tensor(msum[:], msum[:], conv[:, h], ALU.add)
                dve.wait_ge(rms_ok, h + 1)
                dve.reciprocal(rrms[:], rms[:])
                dve.drain()
                dve.tensor_tensor(on[:].rearrange("p (a b) -> p a b", a=TT),
                                  ps_o[:].rearrange("p (a b) -> p a b", a=TT),
                                  rrms[:].unsqueeze(2).broadcast_to((P, TT, P)), ALU.mult
                                  ).then_inc(on_ok, 1)

            head(0, first=True)
            with dve.Fori(1, NH) as h:
                head(h)
            o_low(NH - 1)

            def norm(i, n, src, after):
                dve.drain().then_inc(ln[i]["sum"], 1)
                dve.wait_ge(ln[i]["mean"], 1)
                for k in range(n):
                    dve.scalar_tensor_tensor(src[:, k], ps_x[:], -1.0 / (n * P), src[:, k],
                                             ALU.mult, ALU.add).then_inc(ln[i]["cent"], 1)
                dve.wait_ge(ln[i]["std_ok"], 1)
                dve.reciprocal(rstd[:], std[:])
                dve.drain()
                for k in range(n + 1):
                    if k < n:
                        if k >= 2:
                            dve.wait_ge(ln[i]["affine"], k - 1)
                        dve.tensor_tensor(nrm[:, k % 2], src[:, k], rstd[:], ALU.mult
                                          ).then_inc(ln[i]["scaled"], 1)
                    if k >= 1:
                        dve.wait_ge(ln[i]["hi_ok"], k)
                        after(k - 1)

            def after_conv(k):
                dve.tensor_tensor(swlo[:, k], conv[:, k], swhi[:, k].bitcast(F32), ALU.subtract
                                  ).then_inc(ln[0]["lo_ok"], 1)

            norm(0, NH, conv, after_conv)

            with dve.Fori(0, U2 // 2) as i:
                for s in range(2):
                    dve.wait_ge(gl_in[s], 32 * i + 32)
                    dve.wait_ge(blk_done, 4 * i + (B2 + 2 * s + 2))
                    dve.tensor_tensor(gl[:, s, 0], gl[:, s, 0], ps[2 * s][:], ALU.mult)
                    dve.tensor_tensor(gl[:, s, 1], gl[:, s, 1], ps[2 * s + 1][:], ALU.mult).then_inc(evac2, 1)
                    dve.drain()
                    dve.tensor_tensor(mt[:], gl[:, s, 0], gl[:, s, 1], ALU.add)
                    dve.drain()
                    dve.tensor_copy(ahi[:, 2 * i + s], mt[:])
                    dve.drain()
                    dve.tensor_tensor(alo[:, 2 * i + s], mt[:], ahi[:, 2 * i + s].bitcast(F32),
                                      ALU.subtract).then_inc(mix_ok, 1)

            def residual_pair(i, first=False):
                for s in range(2):
                    dve.wait_ge(xr_in[s], 16 * i + 16)
                    dve.wait_ge(blk_done, 4 * i + (B3 + 2 * s + 2))
                    dve.scalar_tensor_tensor(res[:, 2 * i + s], xr[:, s], ALPHA, ps[s][:],
                                             ALU.mult, ALU.add).then_inc(res_ok, 1)
                    dve.drain()
                    if first and s == 0:
                        dve.tensor_copy(msum[:], res[:, 0])
                    else:
                        dve.tensor_tensor(msum[:], msum[:], res[:, 2 * i + s], ALU.add)

            residual_pair(0, first=True)
            with dve.Fori(1, U3 // 2) as i:
                residual_pair(i)

            def after_ln1(k):
                dve.tensor_tensor(alo[:, k], res[:, k], ahi[:, k].bitcast(F32), ALU.subtract
                                  ).then_inc(ln[1]["lo_ok"], 1)

            norm(1, KD, res, after_ln1)

            def best16(vals, idx, a, b):
                for t in range(TT):
                    dve.max(vals[:, t, 0:8], a[:, t])
                dve.drain()
                for t in range(TT):
                    dve.max_index(idx[:, t, 0:8], vals[:, t, 0:8], a[:, t])
                    dve.match_replace(b[:, t], vals[:, t, 0:8], a[:, t], -3e38)
                dve.drain()
                for t in range(TT):
                    dve.max(vals[:, t, 8:16], b[:, t])
                dve.drain()
                for t in range(TT):
                    dve.max_index(idx[:, t, 8:16], vals[:, t, 8:16], b[:, t])
                dve.drain()

            with dve.Fori(0, PH) as h:
                for cc in range(2):
                    dve.wait_ge(sc_full, 2 * h + cc + 1)
                    dve.tensor_copy(s4[:].rearrange("p a k -> p (a k)"), ps_s[cc][:]).then_inc(sc_free, 1)
                    dve.drain()
                    best16(top[:, cc], topi[:, cc], s4, s4b)
                dve.tensor_copy(k1f[:, :, h], topi[:, 0])
                dve.tensor_copy(k2f[:, :, h], topi[:, 1])
                dve.tensor_tensor(cand[:].rearrange("p t (a b) -> p t a b", a=TOPK),
                                  top[:, 0].unsqueeze(3).broadcast_to((P, TT, TOPK, TOPK)),
                                  top[:, 1].unsqueeze(2).broadcast_to((P, TT, TOPK, TOPK)), ALU.add)
                dve.drain()
                best16(bnow, pnow, cand, cand2)
                dve.tensor_copy(best[:, :, h], bnow[:])
                dve.tensor_copy(bpos[:, :, h], pnow[:])
            dve.drain()

            with dve.Fori(0, PH) as h:
                dve.tensor_copy(pnow[:], bpos[:, :, h])
                dve.tensor_copy(know[:, 0], k1f[:, :, h])
                dve.tensor_copy(know[:, 1], k2f[:, :, h])
                dve.drain()
                dve.tensor_scalar(pab[:, 0], pnow[:], 4, None, ALU.logical_shift_right)
                dve.tensor_scalar(pab[:, 1], pnow[:], 15, None, ALU.bitwise_and)
                dve.drain()
                dve.tensor_copy(pabf[:], pab[:])
                dve.drain()
                for cc, dst in ((0, i1n), (1, i2n)):
                    dve.tensor_tensor(hot[:], pabf[:, cc].unsqueeze(3).broadcast_to((P, TT, TOPK, TOPK)),
                                      iota[:, 0:TOPK].unsqueeze(1).unsqueeze(1).broadcast_to((P, TT, TOPK, TOPK)),
                                      ALU.is_equal)
                    dve.drain()
                    dve.tensor_tensor(hot[:], hot[:],
                                      know[:, cc].unsqueeze(2).broadcast_to((P, TT, TOPK, TOPK)), ALU.mult)
                    dve.drain()
                    dve.tensor_reduce(pick[:], hot[:], AX.X, ALU.add)
                    dve.drain()
                    dve.tensor_copy(dst[:, :, h], pick[:])
            dve.drain()
            rows = best[:].rearrange("p t h k -> p (t h) k")
            grows = gn[:].rearrange("p t h k -> p (t h) k")
            dve.tensor_tensor(grows, rows, rows[:, :, 0:1].broadcast_to((P, TT * PH, TOPK)), ALU.subtract
                              ).then_inc(soft_in, 1)
            dve.wait_ge(soft_exp, 1)
            dve.tensor_reduce(gsum[:], grows, AX.X, ALU.add)
            dve.drain()
            dve.reciprocal(grcp[:], gsum[:])
            dve.drain()
            dve.tensor_tensor(grows, grows, grcp[:].unsqueeze(2).broadcast_to((P, TT * PH, TOPK)), ALU.mult
                              ).then_inc(picks_ok, 1)
            last = TT - 1
            dve.scalar_tensor_tensor(idf[:], i1n[:, last].rearrange("p h k -> p (h k)"), float(NK),
                                     i2n[:, last].rearrange("p h k -> p (h k)"), ALU.mult, ALU.add)
            dve.drain()
            dve.tensor_copy(idx[:], idf[:])
            dve.tensor_copy(gd[:], gn[:, last].rearrange("p h k -> p (h k)"))
            dve.wait_ge(picks_full, 1)
            dve.tensor_copy(ghi[:], ps_s[0][:, 0:TD])
            dve.tensor_copy(i1T[:], ps_s[1][:, 0:TD])
            dve.tensor_copy(i2T[:], ps_x[:, 0:TD])
            dve.drain()
            dve.tensor_tensor(glo[:], ps_s[0][:, 0:TD], ghi[:].bitcast(F32), ALU.subtract)
            dve.drain()

            def one_hots(g, s):
                tok = bass.ds(4 * g, 4)
                for dst, src in ((hot1, i1T), (hot2, i2T)):
                    oh = dve.tensor_tensor(dst[:, s], src[:, tok].unsqueeze(2).broadcast_to((P, 4, P)),
                                           iota[:].unsqueeze(1).broadcast_to((P, 4, P)), ALU.is_equal)
                oh.then_inc(hot_ok, 1)

            def take_group(t, g):
                dve.wait_ge(g_full, GT * t + g + 1)
                for c in range(2):
                    tk = 4 * g + 2 * c
                    tg = dve.tensor_reduce(gst[:].rearrange("p (k t) -> p t k", t=RT)[:, tk:tk + 2, :],
                                           ps_g[g % 2][c][:].rearrange("p (t h k) -> p t k h", t=2, h=2),
                                           AX.X, ALU.add)
                tg.then_inc(g_evac, 1)

            def name_rows(n, s):
                dve.tensor_copy(idxs[:, s, 0:1], idx[:, bass.ds(n, 1)]).then_inc(idx_ok, 1)

            def dot(n, m, s, more=True):
                dve.wait_ge(rows_in[s], 16 * m + 16)
                rows = urows[:, s].rearrange("p (k d) -> p k d", k=KD)
                dve.scalar_tensor_tensor(rows, rows, 1.0, x1n[:, :, TD:T], ALU.mult, ALU.mult,
                                         accum_out=hd[:, bass.ds(n, 1)])
                dve.drain()
                if more:
                    name_rows(n + RING, s)

            def routing_tile(t, first=False):
                n = 0

                def next_dot():
                    nonlocal n
                    dot(NTG * t + n, NTG // RING * t + n // RING, n % RING)
                    n += 1

                for g in range(GT):
                    if g == 2:
                        if first:
                            dve.wait_ge(x1_out, 64)
                        else:
                            dve.wait_ge(tile_out, t * 64)
                    if g >= 2:
                        take_group(t, g - 2)
                    one_hots(GT * t + g, g % 2)
                    if g % 4 != 0:
                        next_dot()
                for g in range(GT - 2, GT):
                    take_group(t, g)
                    next_dot()
                while n < NTG:
                    next_dot()

            for n in range(RING):
                name_rows(n, n)
            dve.wait_ge(x1n_ok, 4)
            routing_tile(0, first=True)
            with dve.Fori(1, NRT) as t:
                routing_tile(t)
            for n in range(NTG * NRT, NP):
                dot(n, n // RING, n % RING, more=n + RING < NP)
            dve.drain().then_inc(dots_ok, 1)

            def expert_weights(g, k, q):
                s = k // 2 % 2
                dve.drain()
                dve.wait_ge(hg_in[s], g * 64 + 32 * (k // 4 + 1))
                dve.tensor_tensor(wt[:].rearrange("p (a t) -> p a t", a=NRT),
                                  hg[:, s, 0, (k % 2) * TD:(k % 2 + 1) * TD].rearrange("p (a t) -> p a t", a=NRT),
                                  hg[:, s, 1].rearrange("p (a c t) -> p c a t", a=NRT, c=2)[:, k % 2], ALU.mult)
                dve.drain()
                dve.tensor_copy(xwhi[q][:, k], wt[:])
                dve.drain()
                dve.tensor_tensor(xwlo[q][:, k], wt[:], xwhi[q][:, k].bitcast(F32), ALU.subtract
                                  ).then_inc(w_ok, 1)

            def add_rows(n, m, s, first=False, more=True):
                dve.drain()
                dve.wait_ge(rows_in[s], 16 * m + (16 + 16 * NP // RING))
                w = hd[:, bass.ds(n, 1)]
                if first:
                    dve.tensor_scalar(yacc[:], vrows[:, s], w, None, ALU.mult)
                else:
                    dve.scalar_tensor_tensor(yacc[:], vrows[:, s], w, yacc[:], ALU.mult, ALU.add)
                dve.drain()
                if more:
                    name_rows(n + RING, s)

            for k in range(8):
                expert_weights(0, k, 0)
            dve.wait_ge(blk_done, B6)
            for n in range(RING):
                name_rows(n, n)
            dve.wait_ge(p_in, 16)
            dve.tensor_copy(phi[:], pin[:])
            dve.drain()
            dve.tensor_tensor(plo[:], pin[:], phi[:].bitcast(F32), ALU.subtract).then_inc(p_ok, 1)
            dve.wait_ge(hd_gelu, 1)
            dve.tensor_tensor(hd[:], hd[:], gd[:], ALU.mult)
            dve.wait_ge(x1_in, 64)

            def add_values(g, q, first=False, last=False):
                for u in range(8):
                    if not last:
                        expert_weights(g + 1, u, 1 - q)
                    dve.wait_ge(blk_done, g * 16 + (B6 + 2 * u + 2))
                    for n in range(2):
                        r = res[:, 2 * u + n, 0:TD]
                        p = ps[2 * (u % 2) + n][:, 0:TD]
                        if first:
                            ad = dve.scalar_tensor_tensor(r, r, ALPHA, p, ALU.mult, ALU.add)
                        else:
                            ad = dve.tensor_tensor(r, r, p, ALU.add)
                    ad.then_inc(evac6, 1)
                    if last:
                        for n in range(2):
                            dve.drain()
                            if u == 0 and n == 0:
                                dve.tensor_copy(msum2[:, 0:TD], res[:, 0, 0:TD])
                            else:
                                dve.tensor_tensor(msum2[:, 0:TD], msum2[:, 0:TD], res[:, 2 * u + n, 0:TD], ALU.add)
                    if first:
                        for n in range(max(0, 2 * (u - 3)), 2 * (u - 2) if 3 <= u < 7 else 0):
                            add_rows(n, n // RING, n % RING, first=(n == 0))
                    else:
                        add_rows(8 * g + u, 2 * g + u // RING, u % RING, more=not (last and u >= RING))

            add_values(0, 0, first=True)
            add_values(1, 1)
            with dve.Fori(1, 7) as i:
                for q in range(2):
                    add_values(2 * i + q, q)
            add_values(14, 0)
            add_values(15, 1, last=True)
            dve.drain().then_inc(yacc_ok, 1)
            dve.wait_ge(yacc_full, 1)
            for q in range(4):
                r = res[:, 4 * q:4 * q + 4, TD:T]
                ya = dve.scalar_tensor_tensor(r, r, ALPHA, ps[4 + q][:].rearrange("p (k t) -> p k t", k=4),
                                              ALU.mult, ALU.add)
                ya.then_inc(yacc_used, 1)
            dve.drain()
            dve.tensor_reduce(msum2[:, TD:T], res[:, :, TD:T].rearrange("p k t -> p t k"), AX.X, ALU.add)

            def after_ln2(k):
                dve.tensor_tensor(alo[:, k], res[:, k], ahi[:, k].bitcast(F32), ALU.subtract
                                  ).then_inc(ln[2]["lo_ok"], 1)

            norm(2, KD, res, after_ln2)

            with dve.Fori(0, U8 // 2) as i:
                for s in range(2):
                    dve.wait_ge(evac8, 2 * i + s + 1)
                    dve.tensor_tensor(sig[:, s], sig[:, s], eT[:, 2 * i + s], ALU.mult)
                    dve.drain()
                    dve.tensor_tensor(yT[:, s], sig[:, s], res[:, 2 * i + s], ALU.add).then_inc(y_ok, 1)


def kernel(**inputs):
    import numpy as np
    import concourse.bacc as bacc
    from concourse.bass_utils import run_bass_kernel_spmd

    a = {k: np.asarray(v) for k, v in inputs.items()}

    def units(w):
        return w.reshape(2, 8, P, -1, P).transpose(3, 2, 0, 1, 4).reshape(-1, P, 2, 1024)

    win = units(a["w_in"][0])
    conv_v, conv_g = win[0:8], win[8:16]
    q, k, v, gates = win[16:24], win[24:32], win[32:40], win[40:72]
    heads = [np.concatenate([q[h:h + 1], k[h:h + 1], v[h:h + 1], conv_v[h:h + 1], conv_g[h:h + 1],
                             gates[3 * h:3 * h + 3]]) for h in range(NH)]
    branch = np.stack([a[n][0].reshape(8, P, KD, P).transpose(2, 1, 0, 3).reshape(KD, P, 1024)
                       for n in ("conv_w_out", "attn_w_o")], axis=2)
    u = a["peer_u"][0].reshape(NK, NK, 2, 8, P).transpose(1, 4, 2, 3, 0).reshape(-1, P, 2, 1024)
    vv = a["peer_v"][0].reshape(NK, 16, 8, 8, 2, P).transpose(1, 3, 0, 4, 2, 5).reshape(-1, P, 2, 1024)
    wp = a["ple_w_proj"][0].reshape(2, P, 2, 2, 4, P).transpose(2, 1, 3, 4, 0, 5).reshape(-1, P, 2, 1024)
    ws = np.concatenate(heads + [gates[FIRST_GATE_TAIL:], branch, units(a["w_out"][0]),
                                 units(a["peer_w_q"][0]), u, vv, wp, units(a["ple_w_gate"][0])])
    assert ws.shape == (NU, P, 2, 1024)
    slopes = 2.0 ** (-8.0 * np.arange(1, NH + 1) / NH)

    def chunks(x):
        return x.reshape(-1, P).T

    cols = [a["conv_dw_w"][0, :, 0].reshape(W, NH, P).transpose(2, 1, 0)]
    cols += [chunks(a[n][0])[:, :, None] for n in ("conv_dw_b", "conv_ln_g", "conv_ln_b")]
    cols.append(np.broadcast_to(slopes.astype(np.float32)[None, :, None], (P, NH, 1)))
    cols.append(np.zeros((P, NH, NCPAR - C_SLOPE - 1), np.float32))
    arrays = {
        "ws": ws,
        "xT": a["x"][0].T.reshape(KD, P, T).transpose(1, 0, 2),
        "pT": a["p"][0, 0].T.reshape(2, P, T).transpose(1, 0, 2),
        "cpar": np.concatenate(cols, axis=2),
        "pvec": np.concatenate([chunks(a[n][0]) for n in ("ln1_g", "ln1_b", "ln2_g", "ln2_b", "ple_b_gate",
                                                          "b_gate", "attn_subln_g")], axis=1),
        "lamT": np.stack([a["attn_lambda_" + n][0] for n in ("q1", "k1", "q2", "k2")], axis=1),
        "u_tab": a["peer_u"][0],
        "v_tab": a["peer_v"][0],
        "keysT": a["peer_sub_keys"][0].reshape(2 * PH, NK, P).transpose(2, 0, 1),
    }
    order = ("ws", "xT", "pT", "cpar", "pvec", "lamT", "keysT", "u_tab", "v_tab")
    arrays = {n: np.ascontiguousarray(arrays[n]) for n in order}
    nc = bacc.Bacc("TRN2", target_bir_lowering=False, num_devices=1)
    args = [nc.dram_tensor(n, x.shape, F32, kind="ExternalInput").ap() for n, x in arrays.items()]
    args.append(nc.dram_tensor("y", (1, T, D), F32, kind="ExternalOutput").ap())
    build(nc, *args)
    r = run_bass_kernel_spmd(nc, [arrays], core_ids=[0])
    return r.results[0]["y"]
```
